# Optimizing a Trainium2 kernel written in Bass

```python
import math
import jax
import jax.numpy as jnp
from jax import lax
import numpy as np
import jax, jax.numpy as jnp

D_MODEL = 1024
BATCH = 1
SEQ = 256
DEPTH = 2

SSD_HEADS = 16
SSD_HEAD_DIM = 64
D_SSD = SSD_HEADS * SSD_HEAD_DIM
SSD_GROUPS = 2
SSD_STATE = 128
SSD_CONV = 4
SSD_CHUNK = 256
CONV_DIM = D_SSD + 2 * SSD_GROUPS * SSD_STATE
ATT_HEADS = 8
ATT_HEAD_DIM = 128
D_ATT = ATT_HEADS * ATT_HEAD_DIM
IDX_HEADS = 8
IDX_HEAD_DIM = 64
TOPK_MAX = 256
Q_BLOCK = 128
ROPE_THETA = 500000.0
ATT_ROPE_DIM = ATT_HEAD_DIM // 4
IDX_ROPE_DIM = IDX_HEAD_DIM // 4
D_MIX = D_SSD + D_ATT
D_FF = 2816
EPS = 1e-6
MIX_SPLITS = (D_SSD, CONV_DIM, SSD_HEADS, D_ATT, D_ATT, D_ATT,
              IDX_HEADS * IDX_HEAD_DIM, IDX_HEAD_DIM, IDX_HEADS)
SPLIT_POINTS = tuple(int(p) for p in np.cumsum(MIX_SPLITS)[:-1])
D_IN_PROJ = sum(MIX_SPLITS)


def rmsnorm(x, g):
    xf = x.astype(jnp.float32)
    y = xf * lax.rsqrt(jnp.mean(xf * xf, axis=-1, keepdims=True) + EPS)
    return (y * g.astype(jnp.float32)).astype(x.dtype)

def swiglu_ffn(x, w_in, w_out):
    gate, up = jnp.split(x @ w_in, 2, axis=-1)
    return (jax.nn.silu(gate) * up) @ w_out

def partial_rope(x, positions, rot_dim):
    inv_freq = ROPE_THETA ** (-jnp.arange(0, rot_dim, 2, dtype=jnp.float32) / rot_dim)
    ang = positions.astype(jnp.float32)[..., None] * inv_freq
    cos = jnp.cos(ang)[:, :, None, :]
    sin = jnp.sin(ang)[:, :, None, :]
    xr = x[..., :rot_dim].astype(jnp.float32)
    x1, x2 = jnp.split(xr, 2, axis=-1)
    rot = jnp.concatenate([x1 * cos - x2 * sin, x2 * cos + x1 * sin], axis=-1)
    return jnp.concatenate([rot.astype(x.dtype), x[..., rot_dim:]], axis=-1)

def causal_dwconv(x, w, b):
    k = w.shape[0]
    y = lax.conv_general_dilated(x, w[:, None, :].astype(x.dtype), window_strides=(1,),
                                 padding=[(k - 1, 0)],
                                 dimension_numbers=('NWC', 'WIO', 'NWC'),
                                 feature_group_count=x.shape[-1])
    return y + b.astype(x.dtype)

def segsum_exp(a):
    l = a.shape[-1]
    cs = jnp.cumsum(a, axis=-1)
    seg = cs[..., :, None] - cs[..., None, :]
    mask = jnp.tril(jnp.ones((l, l), dtype=bool))
    return jnp.exp(jnp.where(mask, seg, -jnp.inf))

def ssd_chunked(xh, dt, a, bmat, cmat, chunk):
    bsz, L, H, P = xh.shape
    G, N = bmat.shape[-2:]
    E = H // G
    nc = L // chunk
    x = (xh.astype(jnp.float32) * dt[..., None]).reshape(bsz, nc, chunk, G, E, P)
    adt = jnp.moveaxis((dt * a).reshape(bsz, nc, chunk, G, E), 2, -1)
    a_cs = jnp.cumsum(adt, axis=-1)
    bc = bmat.astype(jnp.float32).reshape(bsz, nc, chunk, G, N)
    cc = cmat.astype(jnp.float32).reshape(bsz, nc, chunk, G, N)
    decay = segsum_exp(adt)
    cb = jnp.einsum('bclgn,bcsgn->bcgls', cc, bc)
    y_diag = jnp.einsum('bcgls,bcgels,bcsgep->bclgep', cb, decay, x)
    decay_states = jnp.exp(a_cs[..., -1:] - a_cs)
    states = jnp.einsum('bclgn,bcgel,bclgep->bcgepn', bc, decay_states, x)
    chunk_decay = jnp.exp(a_cs[..., -1])

    def step(h, inp):
        st, dec = inp
        return h * dec[..., None, None] + st, h

    h0 = jnp.zeros((bsz, G, E, P, N), jnp.float32)
    _, h_in = lax.scan(step, h0, (jnp.moveaxis(states, 1, 0), jnp.moveaxis(chunk_decay, 1, 0)))
    h_in = jnp.moveaxis(h_in, 0, 1)
    y_off = jnp.einsum('bclgn,bcgepn,bcgel->bclgep', cc, h_in, jnp.exp(a_cs))
    return (y_diag + y_off).reshape(bsz, L, H, P)

def ssd_mixer(z, xbc, dt_raw, conv_w, conv_b, dt_bias, a_log, d_skip, norm_g):
    bsz, L, _ = z.shape
    xbc = jax.nn.silu(causal_dwconv(xbc, conv_w, conv_b))
    xs, bm, cm = jnp.split(xbc, [D_SSD, D_SSD + SSD_GROUPS * SSD_STATE], axis=-1)
    xh = xs.reshape(bsz, L, SSD_HEADS, SSD_HEAD_DIM)
    bm = bm.reshape(bsz, L, SSD_GROUPS, SSD_STATE)
    cm = cm.reshape(bsz, L, SSD_GROUPS, SSD_STATE)
    dt = jax.nn.softplus(dt_raw.astype(jnp.float32) + dt_bias.astype(jnp.float32))
    a = -jnp.exp(a_log.astype(jnp.float32))
    chunk = math.gcd(SSD_CHUNK, L)
    y = ssd_chunked(xh, dt, a, bm, cm, chunk)
    y = y + xh.astype(jnp.float32) * d_skip.astype(jnp.float32)[:, None]
    y = y.reshape(bsz, L, D_SSD) * jax.nn.silu(z.astype(jnp.float32))
    yg = y.reshape(bsz, L, SSD_GROUPS, D_SSD // SSD_GROUPS)
    yg = yg * lax.rsqrt(jnp.mean(yg * yg, axis=-1, keepdims=True) + EPS)
    return (yg.reshape(bsz, L, D_SSD) * norm_g.astype(jnp.float32)).astype(z.dtype)

def dsa_mixer(q, k, v, q_idx, k_idx, w_idx, positions):
    bsz, L, _ = q.shape
    q = partial_rope(q.reshape(bsz, L, ATT_HEADS, ATT_HEAD_DIM), positions, ATT_ROPE_DIM)
    k = partial_rope(k.reshape(bsz, L, ATT_HEADS, ATT_HEAD_DIM), positions, ATT_ROPE_DIM)
    v = v.reshape(bsz, L, ATT_HEADS, ATT_HEAD_DIM)
    qi = partial_rope(q_idx.reshape(bsz, L, IDX_HEADS, IDX_HEAD_DIM), positions, IDX_ROPE_DIM)
    ki = partial_rope(k_idx[:, :, None, :], positions, IDX_ROPE_DIM)[:, :, 0].astype(jnp.float32)
    wi = w_idx.astype(jnp.float32) * IDX_HEADS ** -0.5
    topk = min(TOPK_MAX, L // 4)
    n_blocks = L // Q_BLOCK
    key_pos = jnp.arange(L)
    att_scale = ATT_HEAD_DIM ** -0.5
    idx_scale = IDX_HEAD_DIM ** -0.5

    def block(i):
        start = i * Q_BLOCK
        qb = lax.dynamic_slice_in_dim(q, start, Q_BLOCK, axis=1)
        qib = lax.dynamic_slice_in_dim(qi, start, Q_BLOCK, axis=1)
        wb = lax.dynamic_slice_in_dim(wi, start, Q_BLOCK, axis=1)
        t = start + jnp.arange(Q_BLOCK)
        causal = key_pos[None, :] <= t[:, None]
        logit_idx = jnp.einsum('bthd,bsd->bths', qib.astype(jnp.float32), ki) * idx_scale
        score = jnp.einsum('bth,bths->bts', wb, jax.nn.relu(logit_idx))
        score = jnp.where(causal[None], score, -jnp.inf)
        _, sel = lax.top_k(score, topk)
        k_sel = jax.vmap(lambda kb, ib: kb[ib])(k, sel)
        v_sel = jax.vmap(lambda vb, ib: vb[ib])(v, sel)
        valid = sel <= t[None, :, None]
        s = jnp.einsum('bthd,btkhd->bhtk', qb.astype(jnp.float32),
                       k_sel.astype(jnp.float32)) * att_scale
        s = jnp.where(valid[:, None], s, -jnp.inf)
        p = jax.nn.softmax(s, axis=-1)
        o = jnp.einsum('bhtk,btkhd->bthd', p, v_sel.astype(jnp.float32))
        return o.astype(q.dtype)

    out = lax.map(block, jnp.arange(n_blocks))
    return jnp.moveaxis(out, 0, 1).reshape(bsz, L, D_ATT)

def first_inputs(seed: int = 0) -> dict:
    key = jax.random.key(seed)
    ks = jax.random.split(key, 20)
    f32 = jnp.float32

    def dense(k, shape, fan_in):
        return jax.random.normal(k, shape, f32) * fan_in ** -0.5

    def gain(k, shape):
        return 1.0 + 0.02 * jax.random.normal(k, shape, f32)

    x = jax.random.normal(ks[0], (BATCH, SEQ, D_MODEL), f32)
    offset = jax.random.randint(ks[1], (BATCH, 1), 0, 1024, dtype=jnp.int32)
    positions = (offset + jnp.arange(SEQ, dtype=jnp.int32)[None, :]).astype(jnp.int32)
    dt0 = jnp.exp(jax.random.uniform(ks[10], (DEPTH, SSD_HEADS), f32,
                                     minval=math.log(1e-3), maxval=math.log(1e-1)))
    dt_bias = dt0 + jnp.log(-jnp.expm1(-dt0))
    a_log = jnp.log(jax.random.uniform(ks[11], (DEPTH, SSD_HEADS), f32, minval=1.0, maxval=16.0))
    return {
        'x': x,
        'positions': positions,
        'norm_ffn1': gain(ks[2], (DEPTH, D_MODEL)),
        'w_ffn1_in': dense(ks[3], (DEPTH, D_MODEL, 2 * D_FF), D_MODEL),
        'w_ffn1_out': dense(ks[4], (DEPTH, D_FF, D_MODEL), D_FF),
        'norm_mix': gain(ks[5], (DEPTH, D_MODEL)),
        'w_mix_in': dense(ks[6], (DEPTH, D_MODEL, D_IN_PROJ), D_MODEL),
        'conv_w': dense(ks[7], (DEPTH, SSD_CONV, CONV_DIM), SSD_CONV),
        'conv_b': 0.02 * jax.random.normal(ks[8], (DEPTH, CONV_DIM), f32),
        'dt_bias': dt_bias,
        'a_log': a_log,
        'd_skip': 1.0 + 0.1 * jax.random.normal(ks[9], (DEPTH, SSD_HEADS), f32),
        'ssd_norm': gain(ks[12], (DEPTH, D_SSD)),
        'w_mix_out': dense(ks[13], (DEPTH, D_MIX, D_MODEL), D_MIX),
        'norm_ffn2': gain(ks[14], (DEPTH, D_MODEL)),
        'w_ffn2_in': dense(ks[15], (DEPTH, D_MODEL, 2 * D_FF), D_MODEL),
        'w_ffn2_out': dense(ks[16], (DEPTH, D_FF, D_MODEL), D_FF),
        'final_norm': gain(ks[17], (D_MODEL,)),
    }

def first_block(x, positions, norm_ffn1, w_ffn1_in, w_ffn1_out, norm_mix, w_mix_in,
              conv_w, conv_b, dt_bias, a_log, d_skip, ssd_norm, w_mix_out,
              norm_ffn2, w_ffn2_in, w_ffn2_out, final_norm):
    h = x
    for i in range(DEPTH):
        h = h + 0.5 * swiglu_ffn(rmsnorm(h, norm_ffn1[i]), w_ffn1_in[i], w_ffn1_out[i])
        u = rmsnorm(h, norm_mix[i]) @ w_mix_in[i]
        z, xbc, dt_raw, q, k, v, q_idx, k_idx, w_idx = jnp.split(u, SPLIT_POINTS, axis=-1)
        y_ssd = ssd_mixer(z, xbc, dt_raw, conv_w[i], conv_b[i], dt_bias[i], a_log[i],
                          d_skip[i], ssd_norm[i])
        y_att = dsa_mixer(q, k, v, q_idx, k_idx, w_idx, positions)
        h = h + jnp.concatenate([y_ssd, y_att], axis=-1) @ w_mix_out[i]
        h = h + 0.5 * swiglu_ffn(rmsnorm(h, norm_ffn2[i]), w_ffn2_in[i], w_ffn2_out[i])
    return rmsnorm(h, final_norm)


GRID_W = 64
CTX_LEN = 256
HEAD_DIM = 64
CONV_W = 512
CONV_K = 31
NA_HEADS = 8
NA_W = NA_HEADS * HEAD_DIM
NA_KH_MAX = 8
NA_KW = 16
NA_QCW = 16
NA_KCW = 32
NA_NCB = GRID_W // NA_QCW
GQA_Q_HEADS = 8
GQA_KV_HEADS = 2
GQA_Q_W = GQA_Q_HEADS * HEAD_DIM
GQA_KV_W = GQA_KV_HEADS * HEAD_DIM
N_BRANCH = 3
FFN_HIDDEN = ((8 * D_MODEL + 767) // 768) * 256
ROPE_THETA_2 = 10000.0
NEG = -1e30
IN_SPLITS = (2 * CONV_W, NA_W, NA_W, NA_W, GQA_Q_W, GQA_KV_W, GQA_KV_W, N_BRANCH * D_MODEL)
IN_WIDTH = sum(IN_SPLITS)


def rmsnorm_2(x, g):
    xf = x.astype(jnp.float32)
    y = xf * lax.rsqrt(jnp.mean(xf * xf, axis=-1, keepdims=True) + EPS)
    return (y * g.astype(jnp.float32)).astype(x.dtype)

def layernorm(x, g, b):
    xf = x.astype(jnp.float32)
    mu = jnp.mean(xf, axis=-1, keepdims=True)
    var = jnp.mean(jnp.square(xf - mu), axis=-1, keepdims=True)
    y = (xf - mu) * lax.rsqrt(var + EPS)
    return (y * g.astype(jnp.float32) + b.astype(jnp.float32)).astype(x.dtype)

def modulate(h, shift, scale):
    return h * (1 + scale) + shift

def split_in(p):
    return jnp.split(p, np.cumsum(IN_SPLITS)[:-1].tolist(), axis=-1)

def heads(t, n):
    return t.reshape(t.shape[:-1] + (n, HEAD_DIM))

def axial_rope(x, pos_row, pos_col):
    half = x.shape[-1] // 2
    freqs = jnp.power(ROPE_THETA_2, -jnp.arange(0, half, 2, dtype=jnp.float32) / half)

    def rot(xa, pos):
        ang = pos[:, None] * freqs
        cos = jnp.cos(ang)[None, :, None, :].astype(x.dtype)
        sin = jnp.sin(ang)[None, :, None, :].astype(x.dtype)
        x1, x2 = jnp.split(xa, 2, axis=-1)
        return jnp.concatenate([x1 * cos - x2 * sin, x1 * sin + x2 * cos], axis=-1)

    return jnp.concatenate([rot(x[..., :half], pos_row), rot(x[..., half:], pos_col)], axis=-1)

def conv_branch(a, conv_w, conv_b, ln_g, ln_b, w_out):
    u = a[..., :CONV_W] * jax.nn.sigmoid(a[..., CONV_W:])
    y = lax.conv_general_dilated(
        u, conv_w[:, None, :], window_strides=(1,), padding=[(CONV_K // 2, CONV_K // 2)],
        dimension_numbers=("NWC", "WIO", "NWC"), feature_group_count=CONV_W) + conv_b
    y = jax.nn.silu(layernorm(y, ln_g, ln_b))
    return y @ w_out

def dense_attention(q, k, v):
    B, T, Hq, dh = q.shape
    Hkv = k.shape[2]
    qg = q.reshape(B, T, Hkv, Hq // Hkv, dh) * (dh ** -0.5)
    s = jnp.einsum("bqhgd,bkhd->bhgqk", qg, k).astype(jnp.float32)
    p = jax.nn.softmax(s, axis=-1).astype(v.dtype)
    return jnp.einsum("bhgqk,bkhd->bqhgd", p, v).reshape(B, T, Hq * dh)

def gqa_latent(q, k, v, kc, vc):
    B, S, Hq, dh = q.shape
    Hkv = k.shape[2]
    G = Hq // Hkv
    k_all = jnp.concatenate([k, kc], axis=1)
    v_all = jnp.concatenate([v, vc], axis=1)
    nblk = S // Q_BLOCK
    qb = jnp.moveaxis((q * (dh ** -0.5)).reshape(B, nblk, Q_BLOCK, Hkv, G, dh), 1, 0)

    def one_block(q_blk):
        s = jnp.einsum("bqhgd,bkhd->bhgqk", q_blk, k_all).astype(jnp.float32)
        p = jax.nn.softmax(s, axis=-1).astype(v.dtype)
        return jnp.einsum("bhgqk,bkhd->bqhgd", p, v_all)

    o = lax.map(one_block, qb)
    return jnp.moveaxis(o, 0, 1).reshape(B, S, Hq * dh)

def na_latent(q, k, v, kc, vc, rpb):
    B, S, H, dh = q.shape
    rows = S // GRID_W
    kh = min(NA_KH_MAX, rows)
    q_cols = np.arange(GRID_W).reshape(NA_NCB, NA_QCW)
    key_cols = (np.clip(np.arange(NA_NCB) * NA_QCW - NA_KW // 2, 0, GRID_W - NA_KCW)[:, None]
                + np.arange(NA_KCW))
    win0 = np.clip(q_cols - NA_KW // 2, 0, GRID_W - NA_KW)[..., None]
    kcols = key_cols[:, None, :]
    col_mask = jnp.asarray((kcols >= win0) & (kcols < win0 + NA_KW))
    col_bias_idx = np.clip(kcols - q_cols[..., None] + NA_KW - 1, 0, 2 * NA_KW - 2)
    qg = (q * (dh ** -0.5)).reshape(B, rows, NA_NCB, NA_QCW, H, dh)
    kg = k.reshape(B, rows, GRID_W, H, dh)
    vg = v.reshape(B, rows, GRID_W, H, dh)
    n_loc = kh * NA_KCW

    def one_row(r):
        r0 = jnp.clip(r - kh // 2, 0, rows - kh)
        kb = lax.dynamic_slice_in_dim(kg, r0, kh, axis=1)[:, :, key_cols]
        vb = lax.dynamic_slice_in_dim(vg, r0, kh, axis=1)[:, :, key_cols]
        qr = lax.dynamic_index_in_dim(qg, r, axis=1, keepdims=False)
        drow = r0 + jnp.arange(kh) - r + NA_KH_MAX - 1
        bias = rpb[:, drow][:, :, col_bias_idx].transpose(0, 2, 3, 1, 4)
        s_loc = jnp.einsum("bnqhd,bknchd->bhnqkc", qr, kb).astype(jnp.float32) + bias.astype(jnp.float32)
        s_loc = jnp.where(col_mask[:, :, None, :], s_loc, NEG).reshape(B, H, NA_NCB, NA_QCW, n_loc)
        s_ctx = jnp.einsum("bnqhd,bthd->bhnqt", qr, kc).astype(jnp.float32)
        p = jax.nn.softmax(jnp.concatenate([s_loc, s_ctx], axis=-1), axis=-1).astype(v.dtype)
        p_loc = p[..., :n_loc].reshape(B, H, NA_NCB, NA_QCW, kh, NA_KCW)
        p_ctx = p[..., n_loc:]
        return (jnp.einsum("bhnqkc,bknchd->bnqhd", p_loc, vb)
                + jnp.einsum("bhnqt,bthd->bnqhd", p_ctx, vc))

    o = lax.map(one_row, jnp.arange(rows))
    return jnp.moveaxis(o, 0, 1).reshape(B, S, H * dh)

def merge(br_a, br_b, br_c, gates, w_out):
    ga, gb, gc = jnp.split(gates, N_BRANCH, axis=-1)
    y = jax.nn.sigmoid(ga) * br_a + jax.nn.sigmoid(gb) * br_b + jax.nn.sigmoid(gc) * br_c
    return y @ w_out

def swiglu(h, w_in, w_out):
    gate, up = jnp.split(h @ w_in, 2, axis=-1)
    return (jax.nn.silu(gate) * up) @ w_out

def second_inputs(seed: int = 0) -> dict:
    key = jax.random.key(seed)
    ks = jax.random.split(key, 23)
    L, D = DEPTH, D_MODEL

    def nrm(k, shape, s):
        return jax.random.normal(k, shape, jnp.float32) * s

    return {
        "x": nrm(ks[0], (BATCH, SEQ, D), 1.0),
        "c": nrm(ks[1], (BATCH, D), 1.0),
        "ctx": nrm(ks[2], (BATCH, CTX_LEN, D), 1.0),
        "c_ctx": nrm(ks[3], (D,), 1.0),
        "w_mod": nrm(ks[4], (L, D, 6 * D), 0.5 * D ** -0.5),
        "b_mod": nrm(ks[5], (L, 6 * D), 0.01),
        "norm1_g": 1.0 + nrm(ks[6], (L, D), 0.05),
        "norm2_g": 1.0 + nrm(ks[7], (L, D), 0.05),
        "w_in": nrm(ks[8], (L, D, IN_WIDTH), D ** -0.5),
        "conv_w": nrm(ks[9], (L, CONV_K, CONV_W), CONV_K ** -0.5),
        "conv_b": nrm(ks[10], (L, CONV_W), 0.01),
        "conv_ln_g": 1.0 + nrm(ks[11], (L, CONV_W), 0.05),
        "conv_ln_b": nrm(ks[12], (L, CONV_W), 0.01),
        "w_conv_out": nrm(ks[13], (L, CONV_W, D), CONV_W ** -0.5),
        "na_rpb": nrm(ks[14], (L, NA_HEADS, 2 * NA_KH_MAX - 1, 2 * NA_KW - 1), 0.1),
        "w_na_out": nrm(ks[15], (L, NA_W, D), NA_W ** -0.5),
        "q_norm_g": 1.0 + nrm(ks[16], (L, HEAD_DIM), 0.05),
        "k_norm_g": 1.0 + nrm(ks[17], (L, HEAD_DIM), 0.05),
        "w_gqa_out": nrm(ks[18], (L, GQA_Q_W, D), GQA_Q_W ** -0.5),
        "w_out": nrm(ks[19], (L, D, D), D ** -0.5),
        "w_ffn_in": nrm(ks[20], (L, D, 2 * FFN_HIDDEN), D ** -0.5),
        "w_ffn_out": nrm(ks[21], (L, FFN_HIDDEN, D), FFN_HIDDEN ** -0.5),
        "final_g": 1.0 + nrm(ks[22], (D,), 0.05),
    }

def second_block(x, c, ctx, c_ctx, w_mod, b_mod, norm1_g, norm2_g, w_in, conv_w, conv_b, conv_ln_g,
              conv_ln_b, w_conv_out, na_rpb, w_na_out, q_norm_g, k_norm_g, w_gqa_out, w_out,
              w_ffn_in, w_ffn_out, final_g):
    S = x.shape[1]
    t = jnp.arange(S)
    pos_row = (t // GRID_W).astype(jnp.float32)
    pos_col = (t % GRID_W).astype(jnp.float32)
    silu_c = jax.nn.silu(c)
    silu_cc = jax.nn.silu(c_ctx)
    xc = ctx
    for l in range(DEPTH):
        last = l == DEPTH - 1
        sh1, sc1, g1, sh2, sc2, g2 = jnp.split((silu_c @ w_mod[l] + b_mod[l])[:, None, :], 6, axis=-1)
        csh1, csc1, cg1, csh2, csc2, cg2 = jnp.split(silu_cc @ w_mod[l] + b_mod[l], 6, axis=-1)

        h = modulate(rmsnorm_2(x, norm1_g[l]), sh1, sc1)
        hc = modulate(rmsnorm_2(xc, norm1_g[l]), csh1, csc1)
        a, naq, nak, nav, gq, gk, gv, gates = split_in(h @ w_in[l])
        ac, naqc, nakc, navc, gqc, gkc, gvc, gatesc = split_in(hc @ w_in[l])

        na_kc, na_vc = heads(nakc, NA_HEADS), heads(navc, NA_HEADS)
        g_kc = rmsnorm_2(heads(gkc, GQA_KV_HEADS), k_norm_g[l])
        g_vc = heads(gvc, GQA_KV_HEADS)

        br_a = conv_branch(a, conv_w[l], conv_b[l], conv_ln_g[l], conv_ln_b[l], w_conv_out[l])
        br_b = na_latent(heads(naq, NA_HEADS), heads(nak, NA_HEADS), heads(nav, NA_HEADS),
                         na_kc, na_vc, na_rpb[l]) @ w_na_out[l]
        q = axial_rope(rmsnorm_2(heads(gq, GQA_Q_HEADS), q_norm_g[l]), pos_row, pos_col)
        k = axial_rope(rmsnorm_2(heads(gk, GQA_KV_HEADS), k_norm_g[l]), pos_row, pos_col)
        br_c = gqa_latent(q, k, heads(gv, GQA_KV_HEADS), g_kc, g_vc) @ w_gqa_out[l]
        x = x + g1 * merge(br_a, br_b, br_c, gates, w_out[l])
        x = x + g2 * swiglu(modulate(rmsnorm_2(x, norm2_g[l]), sh2, sc2), w_ffn_in[l], w_ffn_out[l])

        if not last:
            cbr_a = conv_branch(ac, conv_w[l], conv_b[l], conv_ln_g[l], conv_ln_b[l], w_conv_out[l])
            cbr_b = dense_attention(heads(naqc, NA_HEADS), na_kc, na_vc) @ w_na_out[l]
            cq = rmsnorm_2(heads(gqc, GQA_Q_HEADS), q_norm_g[l])
            cbr_c = dense_attention(cq, g_kc, g_vc) @ w_gqa_out[l]
            xc = xc + cg1 * merge(cbr_a, cbr_b, cbr_c, gatesc, w_out[l])
            xc = xc + cg2 * swiglu(modulate(rmsnorm_2(xc, norm2_g[l]), csh2, csc2), w_ffn_in[l], w_ffn_out[l])
    return rmsnorm_2(x, final_g)


def setup_inputs(seed=0):
    out = dict(first_inputs(seed))
    for name, value in second_inputs(seed + 1).items():
        if name != "x":
            out[name + "_2"] = value
    return out


def reference(
    x, positions, norm_ffn1, w_ffn1_in, w_ffn1_out, norm_mix, w_mix_in, conv_w, conv_b, dt_bias,
    a_log, d_skip, ssd_norm, w_mix_out, norm_ffn2, w_ffn2_in, w_ffn2_out, final_norm, c_2,
    ctx_2, c_ctx_2, w_mod_2, b_mod_2, norm1_g_2, norm2_g_2, w_in_2, conv_w_2, conv_b_2,
    conv_ln_g_2, conv_ln_b_2, w_conv_out_2, na_rpb_2, w_na_out_2, q_norm_g_2, k_norm_g_2,
    w_gqa_out_2, w_out_2, w_ffn_in_2, w_ffn_out_2, final_g_2,
):
    x = first_block(
        x, positions, norm_ffn1, w_ffn1_in, w_ffn1_out, norm_mix, w_mix_in, conv_w, conv_b,
        dt_bias, a_log, d_skip, ssd_norm, w_mix_out, norm_ffn2, w_ffn2_in, w_ffn2_out,
        final_norm,
    )
    return second_block(
        x, c_2, ctx_2, c_ctx_2, w_mod_2, b_mod_2, norm1_g_2, norm2_g_2, w_in_2, conv_w_2,
        conv_b_2, conv_ln_g_2, conv_ln_b_2, w_conv_out_2, na_rpb_2, w_na_out_2, q_norm_g_2,
        k_norm_g_2, w_gqa_out_2, w_out_2, w_ffn_in_2, w_ffn_out_2, final_g_2,
    )


_drawn_inputs = setup_inputs


def setup_inputs(seed=0):
    import zlib

    import numpy as np

    out = dict(_drawn_inputs(seed))
    spreads = {}
    factors = {'ssd_norm': 2.9,
     'norm_ffn2': 4.273,
     'final_norm': 2.768,
     'b_mod_2': 4.257,
     'norm1_g_2': 6.229,
     'norm2_g_2': 2.67,
     'conv_b_2': 8.0,
     'conv_ln_g_2': 6.093,
     'conv_ln_b_2': 8.0,
     'na_rpb_2': 8.0,
     'q_norm_g_2': 8.0,
     'k_norm_g_2': 8.0}
    for name, (base, spread) in spreads.items():
        noise = np.random.default_rng([zlib.crc32(name.encode()), seed]).standard_normal(out[name].shape)
        drawn = base * np.exp(spread * noise) if base else spread * noise
        out[name] = jnp.asarray(drawn.astype(out[name].dtype))
    for name, factor in factors.items():
        out[name] = (out[name] * factor).astype(out[name].dtype)
    return out
```

```python
import math
from contextlib import ExitStack

import numpy as np

import concourse.bass as bass
from concourse import mybir
from concourse.alu_op_type import AluOpType as ALU

F32 = mybir.dt.float32
F32R = mybir.dt.float32r
I32 = mybir.dt.int32
FN = mybir.ActivationFunctionType
AX = mybir.AxisListType

P = 128
D = 1024
KD = D // P
SEQ = 256
FF = 2816
EPS = 1e-6
NEG = -1e30
MIX_W = 6232
IN_W = 6400
NA_FAR = 15
FREE_KEY = -3e38
TAKEN = -3.4e38

COLS = {}
_at = 0
for _n, _w in (("norm_ffn1", 16), ("norm_mix", 16), ("norm_ffn2", 16), ("ssd_norm", 16),
               ("conv_w", 96), ("conv_b", 24), ("norm1_g", 16), ("norm2_g", 16), ("b_mod", 96),
               ("conv2_w", 248), ("conv2_b", 8), ("ln_g", 8), ("ln_b", 8), ("c", 8), ("c_ctx", 8)):
    COLS[_n] = _at
    _at += _w
N_COLS = _at
ROWS = {}
_at = 0
for _n, _w in (("dt_bias", 32), ("a_log", 32), ("d_skip", 32), ("q_g", 128), ("k_g", 128)):
    ROWS[_n] = _at
    _at += _w
N_ROWS = _at
CONST = {}
_at = 0
for _n, _w in (("ident", 128), ("upper", 256), ("late", 128), ("head", 16), ("freq", 16),
               ("cos", 128), ("sin", 128), ("one", 1), ("half", 8)):
    CONST[_n] = _at
    _at += _w
N_CONST = _at


def size(ap):
    n = 1
    for s in ap.shape[1:]:
        n *= s
    return n



def mm(out, lhsT, rhs, start, stop):
    n = size(rhs)
    if lhsT.dtype == F32R:
        us = max(0.107, n / 2400 + 0.003)
    else:
        us = max(0.214, n * 4 / 2400)
    return us, lambda e: e.matmul(out, lhsT, rhs, start=start, stop=stop)


def tp(out, in_, ident):
    return 0.109, lambda e: e.transpose(out, in_, ident)


def act(out, in_, func, bias=None, scale=1.0, accum=None):
    us = 0.09 + size(in_) / 1200 + 0.093 * ((bias is not None) + (not isinstance(scale, float)) + (accum is not None))
    kw = {}
    if bias is not None:
        kw["bias"] = bias
    if accum is not None:
        kw["accum_out"] = accum
    return us, (lambda e: e.activation(out, in_, func, scale=scale, **kw)), func


def tt(out, a, b, op):
    return 0.07 + size(out) / 960, lambda e: e.tensor_tensor(out, a, b, op)


def ts(out, a, s1, s2, op0, op1=None, fast=True):
    us = 0.07 + size(out) / (1920 if fast else 960)
    if op1 is None:
        return us, lambda e: e.tensor_scalar(out, a, s1, None, op0)
    return us, lambda e: e.tensor_scalar(out, a, s1, s2, op0, op1)


def stt(out, a, s, b, op0, op1):
    return 0.07 + size(out) / 960, lambda e: e.scalar_tensor_tensor(out, a, s, b, op0, op1)


def cp(out, a, fast=False):
    return 0.07 + size(out) / (1920 if fast else 960), lambda e: e.tensor_copy(out, a)


def pool_pow(out, a, exps):
    return 0.8 + 0.04 * size(out), lambda e: e.tensor_tensor(out, a, exps, ALU.pow)



class Token:
    def __init__(self, eng, t):
        self.eng, self.t, self.sem, self.count, self.wanted = eng, t, None, 0, False


class Ev:

    def __init__(self):
        self.value = None

    def set(self, value):
        self.value = value


class Ring:

    def __init__(self, items):
        self.free = [(i, []) for i in items]
        self.waiting = []


class Op:
    def __init__(self, eng, parts, after):
        self.eng, self.parts, self.after = eng, parts, [t for t in after if t is not None]
        self.us = sum(p[0] for p in parts)
        self.func = parts[0][2] if eng == "ACT" else None


class Either:
    def __init__(self, *ops):
        self.ops = ops


class Get:
    def __init__(self, ring):
        self.ring = ring


class Need:
    def __init__(self, ev):
        self.ev = ev


class Dma:
    def __init__(self, sem, pairs, after, size):
        self.sem, self.pairs, self.after, self.size = sem, pairs, [t for t in after if t is not None], size


class DmaSem:
    def __init__(self, sem):
        self.sem, self.count = sem, 0


def PE(parts, after):
    return Op("PE", parts, after)


def ACT(part, after):
    return Op("ACT", [part], after)


def DVE(part, after):
    return Op("DVE", [part], after)


def POOL(part, after):
    return Op("POOL", [part], after)


TABLE = {FN.Silu: 1, FN.Exp: 2, FN.Tanh: 2, FN.Sin: 3}
SWITCH = 1.3


class Plan:

    def __init__(self):
        self.queues = {e: [] for e in ("PE", "ACT", "DVE", "POOL", "SP")}
        self.clock = dict.fromkeys(self.queues, 0.0)
        self.clock["DMA"] = 0.0
        self.table = None
        self.jobs = []
        self.serial = 0
        self.last = {}
        self.stage = 0

    def spawn(self, gen, bonus=0.5):
        self.serial += 1
        job = [gen, None, bonus, self.serial]
        self.jobs.append(job)
        self._resume(job, None)

    def _resume(self, job, value):
        try:
            job[1] = job[0].send(value)
            if isinstance(job[1], Get):
                job[1].ring.waiting.append(job)
        except StopIteration:
            self.jobs.remove(job)

    def release(self, ring, item, toks):
        ring.free.append((item, toks))

    def _settle(self):
        moved = True
        while moved:
            moved = False
            for job in list(self.jobs):
                r = job[1]
                if isinstance(r, Need) and r.ev.value is not None:
                    self._resume(job, r.ev.value)
                    moved = True
                elif isinstance(r, Get) and r.ring.free and r.ring.waiting[0] is job:
                    r.ring.waiting.pop(0)
                    self._resume(job, r.ring.free.pop(0))
                    moved = True

    def _start(self, op):
        t = self.clock[op.eng if isinstance(op, Op) else "SP"]
        for a in op.after:
            t = max(t, a.t + 0.06)
        if isinstance(op, Op) and op.func in TABLE and TABLE[op.func] != self.table:
            t += SWITCH
        return t

    def run(self):
        while True:
            self._settle()
            best = None
            for job in self.jobs:
                r = job[1]
                if isinstance(r, (Need, Get)):
                    continue
                for op in (r.ops if isinstance(r, Either) else (r,)):
                    start = self._start(op)
                    key = (start - job[2] + (op.us * 0.5 if isinstance(r, Either) else 0), job[3])
                    if best is None or key < best[0]:
                        best = (key, start, job, op)
            if best is None:
                break
            _, start, job, op = best
            if isinstance(op, Dma):
                self.clock["SP"] = start + 0.06 * len(op.pairs)
                self.clock["DMA"] = max(self.clock["DMA"], start) + op.size / 358e3
                tok = Token("DMA", self.clock["DMA"] + 1.8)
                op.sem.count += 16 * len(op.pairs)
                tok.sem, tok.count = op.sem, op.sem.count
                self.queues["SP"].append((op, tok))
            else:
                tok = Token(op.eng, start + op.us)
                self.clock[op.eng] = tok.t
                if op.func in TABLE:
                    self.table = TABLE[op.func]
                tok.sem = self.stage
                self.queues[op.eng].append((op, tok))
                self.last[op.eng] = tok
            self._resume(job, tok)
        if self.jobs:
            raise RuntimeError("jobs left: " + ", ".join(j[0].__name__ for j in self.jobs))

    def ends(self):
        return list(self.last.values())

    def emit(self, nc, sem_of, final):
        for q in self.queues.values():
            for op, _ in q:
                for a in op.after:
                    a.wanted = True
        for eng, q in self.queues.items():
            if eng == "SP":
                continue
            counts = {}
            for _, tok in q:
                if tok.wanted:
                    counts[tok.sem] = counts.get(tok.sem, 0) + 1
                    tok.count = counts[tok.sem]
                    tok.sem = sem_of(eng, tok.sem)
        def feed(eng):
            def run(e):
                seen = {}

                def wait(a):
                    sem = a.sem.sem if isinstance(a.sem, DmaSem) else a.sem
                    if seen.get(id(sem), 0) < a.count:
                        e.wait_ge(sem, a.count)
                        seen[id(sem)] = a.count
                for op, tok in self.queues[eng]:
                    for a in sorted(op.after, key=lambda a: -a.count):
                        wait(a)
                    if isinstance(op, Dma):
                        for out, in_ in op.pairs:
                            e.dma_start(out, in_).then_inc(op.sem.sem, 16)
                    else:
                        for part in op.parts:
                            ins = part[1](e)
                        if tok.wanted:
                            ins.then_inc(tok.sem, 1)
                if eng == "SP":
                    for tok in final:
                        wait(tok)
            return run
        with nc.Block() as block:
            block.sync(feed("SP"))
            block.scalar(feed("ACT"))
            block.vector(feed("DVE"))
            block.gpsimd(feed("POOL"))
            block.tensor(feed("PE"))



class Sub:

    def __init__(self, k0, nk, nc, at):
        self.k0, self.nk, self.nc, self.at = k0, nk, nc, at
        self.ready = Ev()


class Piece:
    def __init__(self, sources, subs):
        self.sources, self.subs = sources, subs
        self.loaded = Ev()


class Lhs:

    def __init__(self, hi, lo):
        self.hi, self.lo = hi, lo
        self.ready = {}
        self.free = []

    def at(self, k, t0):
        return self.hi[:, k, t0:t0 + P], self.lo[:, k, t0:t0 + P]

    def ev(self, k, g=0):
        return self.ready.setdefault((k, g), Ev())


class Both(Lhs):

    def __init__(self, a, b):
        super().__init__(None, None)
        self.a, self.b = a, b

    def at(self, k, t0):
        return self.a.at(k, t0) if k < 8 else self.b.at(k - 8, t0)


class Residual:
    def __init__(self, tile):
        self.tile = tile
        self.written = [[Ev(), Ev()], [Ev(), Ev()]]
        self.readers = [[], []]

    def renew(self):
        old, self.readers = self.readers, [[], []]
        before = self.written
        self.written = [[Ev(), Ev()], [Ev(), Ev()]]
        return old, before


def program(nc, A, out, scratch):
    ctx = ExitStack()
    with ctx:
        sems = {}

        def sem_of(eng, stage):
            if (eng, stage) not in sems:
                sems[eng, stage] = ctx.enter_context(nc.semaphore(f"{eng.lower()}_{stage}"))
            return sems[eng, stage]

        def dma_sem(name):
            return DmaSem(ctx.enter_context(nc.semaphore(name)))

        plan = Plan()
        spawn, release = plan.spawn, plan.release
        place = [nc.sbuf_base]
        limit = 229344

        def tile(name, shape, dt=F32, at=None):
            n = 4
            for v in shape[1:]:
                n *= v
            n = (n + 31) // 32 * 32
            where = place if at is None else at
            where[0] = (where[0] + 31) // 32 * 32
            t = nc.alloc_sbuf_tensor_at(name, list(shape), dt, offset=where[0])
            where[0] += n
            if where[0] > limit:
                raise RuntimeError(f"{name} ends at {where[0]}")
            return t

        ps = ctx.enter_context(nc.psum_tensor("ps", [P, 8, 512], F32))
        MAIN = Ring([0, 1, 2, 3])
        SIDE = Ring([4, 5, 6, 7])

        raw = tile("raw", [P, 4, 2048])
        whi = tile("whi", [P, 4, 1024], F32R)
        wlo = tile("wlo", [P, 4, 1024], F32R)
        h_t = tile("h_t", [P, 2, D])
        hc_at = place[0]
        hc_t = tile("hc_t", [P, 2, D])
        xt_hi = tile("xt_hi", [P, KD, SEQ], F32R)
        xt_lo = tile("xt_lo", [P, KD, SEQ], F32R)
        const = tile("const", [P, N_CONST])
        cols = tile("cols", [P, N_COLS])
        rows = tile("rows", [P, N_ROWS])
        pos_i = tile("pos_i", [P, 2], I32)
        ident_r = tile("ident_r", [P, P], F32R)
        late_r = tile("late_r", [P, P], F32R)
        head_r = tile("head_r", [48, 16], F32R)
        cos_a = tile("cos_a", [P, 2, 2, 16])
        sin_a = tile("sin_a", [P, 2, 2, 16])
        cos_i = tile("cos_i", [P, 2, 2, 8])
        sin_i = tile("sin_i", [P, 2, 2, 8])
        neg_a = tile("neg_a", [P, 32])
        modc = tile("modc", [P, 2, 2, 4, KD])
        gain = tile("gain", [P, 2, 2, 2, KD])
        sc_t = tile("sc_t", [P, 2, KD])
        stat_t = tile("stat_t", [P, 16, 8])
        norm_t = tile("norm_t", [P, 4, 512])
        mod_t = tile("mod_t", [P, 3, 256])
        mod_at = place[0]
        mod_w = tile("mod_w", [P, 2, 512])
        mod_acc = tile("mod_acc", [P, 2, 512])
        mod_row = tile("mod_row", [1, 512])
        phase = place[0]

        def cst(name, n=None, rows_=P):
            a = CONST[name]
            return const[0:rows_, a:a + n]

        ident = cst("ident", 128)
        upper = cst("upper", 256)
        ones = const[:, CONST["one"]:CONST["one"] + 1]

        def col(name, i=0):
            a = COLS[name] + i
            return cols[:, a:a + 1]

        def minus_half(n):
            return const[:, CONST["half"]:CONST["half"] + n]

        raw_ring, hi_ring, lo_ring = Ring([0, 1, 2, 3]), Ring([0, 1, 2, 3]), Ring([0, 1, 2, 3])
        raw_sems = [dma_sem(f"raw{i}") for i in range(4)]
        pieces = []

        def piece(sources, subs):
            p = Piece(sources, subs)
            pieces.append(p)
            return subs

        def w_at(w, layer, k, nk, c, n):
            a = w[layer]
            return a[k * P:(k + nk) * P, c:c + n].rearrange("(k p) n -> p k n", p=P)

        def block_512(w, layer, nk, c, k0=0, local=0):
            subs = []
            k = 0
            while k < nk:
                n = min(4, nk - k)
                subs += piece([(0, n, 512, 512, w_at(w, layer, k0 + k, n, c, 512))],
                              [Sub(local + k + i, min(2, n - i), 512, i * 512) for i in range(0, n, 2)])
                k += n
            return subs

        def block_256(w, layer, c):
            return piece([(0, 8, 256, 256, w_at(w, layer, 0, 8, c, 256))], [Sub(0, 4, 256, 0), Sub(4, 4, 256, 1024)])

        def block_gqa(w, layer, c):
            a = w[layer]
            return piece([(0, 4, 512, 512, a[256 * g:256 * g + 256, c:c + 512].rearrange("(k p) n -> p k n", p=64), 64 * g, 64 * g + 64)
                          for g in range(2)], [Sub(0, 2, 512, 0), Sub(2, 2, 512, 1024)])

        def block_pair(w, layer, c1, c2):
            subs = []
            for k in (0, 4):
                subs += piece([(0, 4, 256, 512, w_at(w, layer, k, 4, c1, 256)),
                               (256, 4, 256, 512, w_at(w, layer, k, 4, c2, 256))],
                              [Sub(k, 2, 512, 0), Sub(k + 2, 2, 512, 1024)])
            return subs

        def loader():
            for p in pieces:
                slot, free = yield Get(raw_ring)
                pairs, total = [], 0
                for off, nk, n, pitch, src, *part in p.sources:
                    p0, p1 = part or (0, P)
                    dst = raw[p0:p1, slot, 0:nk * pitch].rearrange("p (k c) -> p k c", k=nk)[:, :, off:off + n]
                    pairs.append((dst, src))
                    total += nk * n * 4 * (p1 - p0)
                tok = yield Dma(raw_sems[slot], pairs, free, total)
                p.loaded.set((slot, tok))

        def splitter():
            for p in pieces:
                slot, arrived = yield Need(p.loaded)
                for i, s in enumerate(p.subs):
                    n = s.nk * s.nc
                    src = raw[:, slot, s.at:s.at + n]
                    a, free_a = yield Get(hi_ring)
                    t_hi = yield ACT(act(whi[:, a, 0:n], src, FN.Copy), [arrived] + free_a)
                    ev = Ev()
                    spawn(low_part(p, s, i, slot, src, a, t_hi, arrived), bonus=0.7)

        low_order = [Ev()]
        low_order[0].set(True)

        def low_part(p, s, i, slot, src, a, t_hi, arrived):
            mine, after_me = low_order[0], Ev()
            low_order[0] = after_me
            yield Need(mine)
            n = s.nk * s.nc
            b, free_b = yield Get(lo_ring)
            t_lo = yield DVE(tt(wlo[:, b, 0:n], src, whi[:, a, 0:n].bitcast(F32), ALU.subtract), [t_hi, arrived] + free_b)
            s.ready.set((a, b, t_hi, t_lo))
            after_me.set(True)
            if i == len(p.subs) - 1:
                release(raw_ring, slot, [t_hi, t_lo])

        def gemm(subs, lhs, done):
            banks = {}
            for i, s in enumerate(subs):
                a, b, t_hi, t_lo = yield Need(s.ready)
                used = []
                for th, (l, g, half) in enumerate(lhs):
                    after = [t_hi, t_lo]
                    if i == 0:
                        banks[th], free = yield Get(MAIN)
                        after += free
                    parts = []
                    o = ps[:, banks[th], 0:s.nc]
                    t0 = (2 * g + half) * P
                    for k in range(s.nk):
                        after += (yield Need(l.ev(s.k0 + k, g)))
                        x_hi, x_lo = l.at(s.k0 + k, t0)
                        w_hi, w_lo = (x[:, r, k * s.nc:(k + 1) * s.nc] for x, r in ((whi, a), (wlo, b)))
                        first = i == 0 and k == 0
                        last = s is subs[-1] and k == s.nk - 1
                        parts += [mm(o, x_hi, w_hi, first, False), mm(o, x_hi, w_lo, False, False),
                                  mm(o, x_lo, w_hi, False, last)]
                    tok = yield PE(parts, after)
                    used.append(tok)
                    if s is subs[-1]:
                        done[th].set((banks[th], tok))
                release(hi_ring, a, [used[-1]])
                release(lo_ring, b, [used[-1]])

        def fresh(n):
            return [Ev() for _ in range(n)]

        norm_ring = Ring([0, 1, 2, 3])
        modt_ring = Ring([0, 1, 2])
        n_stats = [0]

        def stats(res):
            i = n_stats[0]
            n_stats[0] += 1
            part, mean, rstd = stat_t[:, i, 0:4], stat_t[:, i, 4:6], stat_t[:, i, 6:8]
            got, written, readers = Ev(), res.written, res.readers
            parts_done = fresh(4)

            def one(n, th):
                t = yield Need(written[n][th])
                s, free = yield Get(norm_ring)
                j = 2 * n + th
                tok = yield ACT(act(norm_t[:, s, :], res.tile[:, th, n * 512:(n + 1) * 512], FN.Square,
                                    scale=1.0 / 32, accum=part[:, j:j + 1]), [t] + free)
                release(norm_ring, s, [tok])
                readers[n].append(tok)
                parts_done[j].set(tok)

            def rest():
                toks = []
                for e in parts_done:
                    toks.append((yield Need(e)))
                t = yield DVE(stt(mean, part[:, 0:2], EPS, part[:, 2:4], ALU.add, ALU.add), toks)
                t = yield POOL(pool_pow(rstd, mean, minus_half(2)), [t])
                got.set((rstd, t))
            for n in range(2):
                for th in range(2):
                    spawn(one(n, th))
            spawn(rest(), bonus=1.0)
            return got

        def prep_scaled(res, gains, lhs, free):
            written, readers = res.written, res.readers

            def one(b):
                n = b // 2
                t_c = yield Need(ready["cols"])
                t_k = yield Need(ready["const"])
                t0 = yield Need(written[n][0])
                t1 = yield Need(written[n][1])
                bank, bfree = yield Get(SIDE)
                v = ps[:, bank, :].rearrange("p (k t) -> p k t", k=2)
                tr = yield PE([tp(v[:, j, th * P:(th + 1) * P], res.tile[:, th, (2 * b + j) * P:(2 * b + j + 1) * P], ident)
                               for j in range(2) for th in range(2)], [t0, t1, t_k] + bfree)
                readers[n].append(tr)
                last = []
                for j in range(2):
                    k = 2 * b + j
                    last.append((yield ACT(act(lhs.hi[:, k, 0:SEQ], v[:, j, :], FN.Copy, scale=col(gains[0], gains[1] + k)), [tr, t_c] + free)))
                for j in range(2):
                    k = 2 * b + j
                    c = yield DVE(stt(lhs.lo[:, k, 0:SEQ], v[:, j, :], col(gains[0], gains[1] + k), lhs.hi[:, k, 0:SEQ].bitcast(F32),
                                      ALU.mult, ALU.subtract), [last[0], last[1], t_c] + free)
                    lhs.ev(k).set([last[j], c])
                    last.append(c)
                release(SIDE, bank, last)
            for b in range(4):
                spawn(one(b), bonus=1.0)

        def add_back(res, old, before, n, th, done, factor=None, rows_=None):
            written = res.written
            bank, tok = yield Need(done)
            prev = yield Need(before[n][th])
            dst = res.tile[:, th, n * 512:(n + 1) * 512]
            if rows_ is None:
                t = yield DVE(stt(dst, ps[:, bank, :], factor, dst, ALU.mult, ALU.add), [tok, prev] + old[n])
                release(MAIN, bank, [t])
            else:
                row, t_row = rows_
                m = yield DVE(tt(ps[:, bank, :], ps[:, bank, :], row[:, n * 512:(n + 1) * 512], ALU.mult), [tok, t_row])
                t = yield DVE(tt(dst, ps[:, bank, :], dst, ALU.add), [m, prev] + old[n])
                release(MAIN, bank, [t])
            written[n][th].set(t)

        def transposed_pair(srcs, toks, emit_rest):
            bank, bfree = yield Get(SIDE)
            v = ps[:, bank, :].rearrange("p (k t) -> p k t", k=2)
            tr = yield PE([tp(v[:, j, th * P:(th + 1) * P], srcs[j][th], ident)
                           for j in range(len(srcs)) for th in range(2)], toks + bfree)
            last = yield from emit_rest(v, tr)
            release(SIDE, bank, last)
            return tr

        def split_rest(lhs, k, g, scale=1.0):
            def rest(v, tr):
                t0 = g * SEQ
                hi, lo = (x[:, k:k + 2, t0:t0 + SEQ] for x in (lhs.hi, lhs.lo))
                a = yield ACT(act(hi, v, FN.Copy, scale=scale), [tr] + lhs.free)
                if scale == 1.0:
                    c = yield DVE(tt(lo, v, hi.bitcast(F32), ALU.subtract), [a] + lhs.free)
                else:
                    c = yield DVE(stt(lo, v, scale, hi.bitcast(F32), ALU.mult, ALU.subtract), [a] + lhs.free)
                lhs.ev(k, g).set([a, c])
                lhs.ev(k + 1, g).set([a, c])
                return [a, c]
            return rest

        def copy_either(out_, in_, after, scale=None):
            if scale is None:
                return Either(ACT(act(out_, in_, FN.Copy), after), DVE(cp(out_, in_), after))
            return Either(ACT(act(out_, in_, FN.Copy, scale=scale), after),
                          DVE(ts(out_, in_, scale, None, ALU.mult, fast=False), after))

        def ffn(blocks, w_out_subs, groups, parts, n_stage, then):
            at = [phase]
            nk = max(2 * (c1 - c0) for c0, c1 in parts)
            ng = len(groups)
            hid = Lhs(tile(f"hid_hi{n_stage}", [P, nk, SEQ * ng], F32R, at), tile(f"hid_lo{n_stage}", [P, nk, SEQ * ng], F32R, at))
            hid.free = plan.ends()
            begin = plan.ends()
            s_t, u_t = tile(f"s_t{n_stage}", [P, 4, 256], F32, at), tile(f"u_t{n_stage}", [P, 4, 256], F32, at)
            s_ring, u_ring = Ring([0, 1, 2, 3]), Ring([0, 1, 2, 3])
            s_ring.free = [(i, begin) for i in range(4)]
            u_ring.free = [(i, begin) for i in range(4)]
            for (c0, c1), down in zip(parts, w_out_subs):
                def hidden(c, g, done, rstd_ev):
                    made = []
                    slots = []
                    for th in range(2):
                        bank, tok = yield Need(done[2 * g + th])
                        s, sfree = yield Get(s_ring)
                        u, ufree = yield Get(u_ring)
                        if rstd_ev is not None:
                            rstd, t_r = yield Need(rstd_ev)
                            r = rstd[:, th:th + 1]
                            a = yield ACT(act(s_t[:, s, :], ps[:, bank, 0:256], FN.Silu, scale=r), [tok, t_r] + sfree)
                            b = yield DVE(stt(u_t[:, u, :], ps[:, bank, 256:512], r, s_t[:, s, :], ALU.mult, ALU.mult),
                                          [tok, t_r, a] + ufree)
                        else:
                            a = yield ACT(act(s_t[:, s, :], ps[:, bank, 0:256], FN.Silu), [tok] + sfree)
                            b = yield DVE(tt(u_t[:, u, :], ps[:, bank, 256:512], s_t[:, s, :], ALU.mult), [tok, a] + ufree)
                        release(MAIN, bank, [a, b])
                        release(s_ring, s, [b])
                        made.append(b)
                        slots.append(u)
                    tr = yield from transposed_pair(
                        [[u_t[:, slots[th], j * P:(j + 1) * P] for th in range(2)] for j in range(2)],
                        made, split_rest(hid, 2 * (c - c0), g))
                    for u in slots:
                        release(u_ring, u, [tr])
                for c in range(c0, c1):
                    done = fresh(2 * ng)
                    for g in range(ng):
                        spawn(hidden(c, g, done, groups[g][3]))
                    yield from gemm(blocks[c], [(l, g, th) for l, g, *_ in groups for th in range(2)], done)
                renewed = [gr[2].renew() for gr in groups]
                for n in range(2):
                    done = fresh(2 * ng)
                    for g, gr in enumerate(groups):
                        for th in range(2):
                            spawn(add_back(gr[2], renewed[g][0], renewed[g][1], n, th, done[2 * g + th], gr[4], gr[5]), bonus=1.0)
                    if n == 0 and (c0, c1) == parts[-1]:
                        then()
                    yield from gemm(down[n], [(hid, g, th) for g in range(ng) for th in range(2)], done)
                hid.ready = {}
                hid.free = [plan.last["PE"]]

        ready = {n: Ev() for n in ("const", "cols", "rows", "pos", "x", "ctx", "ident_r", "late_r", "head_r", "rope", "neg_a")}

        def setup():
            for name, dst, src in (("cols", cols[:, :], A["cols"]), ("const", const[:, :], A["const"]),
                                   ("pos", pos_i[:, :], A["pos"]),
                                   ("rows", rows[:, :], bass.AP(A["rows"].tensor, 0, ap=[[0, P], [1, N_ROWS]]))):
                t = yield Dma(dma_sem("in_" + name), [(dst, src)], [], 4 * P * size(dst))
                ready[name].set(t)

        def setup_x():
            for n in range(2):
                t = yield Dma(dma_sem(f"in_x{n}"), [(h_t[:, :, n * 512:(n + 1) * 512],
                                                     A["x"][:, n * 512:(n + 1) * 512].rearrange("(t p) n -> p t n", p=P))], [], 1 << 19)
                for th in range(2):
                    h.written[n][th].set(t)

        def setup_small():
            c = yield Need(ready["const"])
            t = yield ACT(act(ident_r[:, :], ident, FN.Copy), [c])
            ready["ident_r"].set(t)
            t = yield ACT(act(late_r[:, :], cst("late", 128), FN.Copy), [c])
            ready["late_r"].set(t)
            t = yield ACT(act(head_r[:, :], const[0:48, CONST["head"]:CONST["head"] + 16], FN.Copy), [c])
            ready["head_r"].set(t)
            r = yield Need(ready["rows"])
            a = ROWS["a_log"]
            t = yield ACT(act(neg_a[:, :], rows[:, a:a + 32], FN.Exp), [r])
            t = yield DVE(ts(neg_a[:, :], neg_a[:, :], -1.0, None, ALU.mult), [t])
            ready["neg_a"].set(t)

        def rope_tables():
            at = [limit - 1024]
            pf = tile("rp_p", [P, 2], F32, at)
            ang, turn, red, ab = (tile(f"rp_{n}", [P, 2, 16], F32, at) for n in "atrb")
            c = yield Need(ready["const"])
            p = yield Need(ready["pos"])
            t = yield DVE(cp(pf[:, :], pos_i[:, :]), [p])
            tk = []
            for th in range(2):
                tk.append((yield DVE(ts(ang[:, th, :], cst("freq", 16), pf[:, th:th + 1], None, ALU.mult), [t, c])))
            magic = 1.5 * 2.0 ** 23
            t = yield DVE(ts(turn[:, :, :], ang[:, :, :], 1.0 / (2 * math.pi), magic, ALU.mult, ALU.add), tk)
            t = yield DVE(ts(turn[:, :, :], turn[:, :, :], magic, None, ALU.subtract), [t])
            c1 = 6.28125
            c2 = float(np.float32(np.round((2 * math.pi - c1) * 2 ** 21) / 2 ** 21))
            c3 = 2 * math.pi - c1 - c2
            src = ang
            for cc in (c1, c2, c3):
                t = yield DVE(stt(red[:, :, :], turn[:, :, :], -cc, src[:, :, :], ALU.mult, ALU.add), [t] + tk)
                src = red
            t = yield DVE(ts(red[:, :, :], red[:, :, :], -3.1415925, 3.1415925, ALU.max, ALU.min), [t])
            b = yield DVE(stt(ab[:, :, :], red[:, :, :], -1.0, red[:, :, :], ALU.mult, ALU.max), [t])
            b = yield DVE(ts(ab[:, :, :], ab[:, :, :], -1.0, math.pi / 2, ALU.mult, ALU.add), [b])
            s = yield ACT(act(sin_a[:, :, 1, :], red[:, :, :], FN.Sin), [t])
            m = yield ACT(act(sin_a[:, :, 0, :], red[:, :, :], FN.Sin, scale=-1.0), [t])
            c = yield ACT(act(cos_a[:, :, 0, :], ab[:, :, :], FN.Sin), [b])
            d = yield DVE(cp(cos_a[:, :, 1, :], cos_a[:, :, 0, :]), [c])
            e = yield DVE(cp(cos_i[:, :, :, :], cos_a[:, :, :, 0:16:2]), [c, d])
            f = yield DVE(cp(sin_i[:, :, :, :], sin_a[:, :, :, 0:16:2]), [s, m])
            ready["rope"].set([c, d, e, f, s, m])

        h, hc = Residual(h_t), Residual(hc_t)

        def swapped(base, dims, r):
            return bass.AP(base.tensor, base.offset + r, ap=[list(base.ap[0])] + dims + [[-r, 2], [1, r]])

        def straight(base, dims, r):
            return bass.AP(base.tensor, base.offset, ap=[list(base.ap[0])] + dims + [[r, 2], [1, r]])

        MIX = dict(z=0, xbc=1024, dt=2560, q=2576, k=3600, v=4624, qidx=5648, kidx=6160)

        def mix1_blocks(i):
            w = A["w_mix_in"]
            b = {}
            b["qidx"] = block_512(w, i, 8, MIX["qidx"])
            b["misc"] = piece([(0, 8, 72, 88, w_at(w, i, 0, 8, MIX["kidx"], 72)),
                               (72, 8, 16, 88, w_at(w, i, 0, 8, MIX["dt"], 16))], [Sub(0, 8, 88, 0)])
            for n, c in (("q", "q"), ("k", "k")):
                for j in range(2):
                    b[n, j] = block_512(w, i, 8, MIX[c] + 512 * j)
            for j in (2, 0, 1):
                b["xbc", j] = block_512(w, i, 8, MIX["xbc"] + 512 * j)
            for j in range(2):
                b["v", j] = block_512(w, i, 8, MIX["v"] + 512 * j)
            for j in range(2):
                b["z", j] = block_512(w, i, 8, MIX["z"] + 512 * j)
            for n in range(2):
                b["out", n] = block_512(A["w_mix_out"], i, 8, 512 * n, 8, 8) + block_512(A["w_mix_out"], i, 8, 512 * n)
            return b

        def mix1(i, b, xt, rstd_ev, then):
            at = [phase]
            begin = plan.ends()
            nm = f"m{i}_"

            def T(name, shape, dt=F32):
                return tile(nm + name, shape, dt, at)

            def ring(n):
                r = Ring(list(range(n)))
                r.free = [(j, begin) for j in range(n)]
                return r
            qk_at = at[0]
            qT, kT = T("qT", [P, 8, SEQ]), T("kT", [P, 8, SEQ])
            at[0] = qk_at
            ssd = Lhs(T("ssd_hi", [P, 8, SEQ], F32R), T("ssd_lo", [P, 8, SEQ], F32R))
            attl = Lhs(T("att_hi", [P, 8, SEQ], F32R), T("att_lo", [P, 8, SEQ], F32R))
            v_t = T("v", [P, 2, D])
            x_t = T("xs", [P, 2, D])
            bc = T("bc", [P, 4, SEQ])
            tok_t, tok_ring = tile(nm + "tok", [P, 4, 512], F32, [hc_at]), ring(4)
            wi, dtv, adt = T("wi", [P, 2, 8]), T("dtv", [P, 2, 16]), T("adt", [P, 2, 16])
            nacs = T("nacs", [P, 2, 16])
            rt, rt_ring = T("rt", [P, 2, 2, 128]), ring(2)
            bias0, bias1 = T("bias0", [P, 128]), T("bias1", [P, 256])
            pr, pr_ring = T("pr", [P, 3, 384]), ring(3)
            prs, prs_ring = T("prs", [P, 3, 8]), ring(3)
            pT, pT_ring = T("pT", [P, 2, 384]), ring(2)
            cin, cin_ring = T("cin", [P, 4, 3 + SEQ]), ring(1)
            cout, cout_ring = T("cout", [P, 4, SEQ]), ring(1)
            acs_f, acs_r = T("acs_f", [16, SEQ]), T("acs_r", [48, 384], F32R)
            al = [at[0]]
            qiT, kiT, kit = (tile(nm + n, s, F32, al) for n, s in (("qiT", [P, 4, SEQ]), ("kiT", [P, SEQ]), ("kit", [P, 2, 128])))
            rl, rl_ring = tile(nm + "rl", [P, 2, 512], F32, al), ring(2)
            sc0, sc1, wk, m8 = (tile(nm + n, s, F32, al) for n, s in (("sc0", [P, 128]), ("sc1", [P, 256]), ("wk", [P, 256]), ("m8", [P, 2, 8])))
            cbT = T("cbT", [P, 2, 384])
            dec, dec_ring = T("dec", [P, 2, 384]), ring(2)
            mt, mt_ring = T("mt", [P, 2, 384]), ring(2)
            zt, zt_ring = T("zt", [P, 2, 512]), ring(2)
            gs = T("gs", [P, 2, 2, 2])

            E = {n: Ev() for n in ("wi0", "wi1", "turn", "dt", "kiT", "qiT0", "qiT1", "index", "bc", "cb0", "cb1", "acs", "x0", "x1",
                                   "bias0", "bias1", "dtraw")}
            q_ready, k_ready, v_ready = fresh(8), fresh(8), [fresh(2), fresh(2)]

            def rope_in_place(buf, nh, hd, r, cos_, sin_, th, tok):
                s, free = yield Get(rt_ring)
                n = nh * 2 * r
                ta, tb = (rt[:, s, j, 0:n].rearrange("p (h s r) -> p h s r", h=nh, s=2) for j in range(2))
                shape = [P, nh, 2, r]
                table = yield Need(ready["rope"])
                c = cos_[:, th, :, :].unsqueeze(1).to_broadcast(shape)
                sn = sin_[:, th, :, :].unsqueeze(1).to_broadcast(shape)
                a = yield DVE(tt(ta, straight(buf, [[hd, nh]], r), c, ALU.mult), [tok] + table + free)
                b_ = yield DVE(tt(tb, swapped(buf, [[hd, nh]], r), sn, ALU.mult), [tok] + table + free)
                d = yield DVE(tt(straight(buf, [[hd, nh]], r), ta, tb, ALU.add), [a, b_])
                release(rt_ring, s, [d])
                return d

            def to_tokens(done, th, scaled=True):
                bank, tok = yield Need(done[th])
                rstd, t_r = yield Need(rstd_ev)
                s, free = yield Get(tok_ring)
                t = yield copy_either(tok_t[:, s, :], ps[:, bank, :], [tok, t_r] + free, scale=rstd[:, th:th + 1])
                release(MAIN, bank, [t])
                return s, t

            def heads_T(done, nh, hd, r, cos_, sin_, dst, evs):
                slots, toks = [], []
                for th in range(2):
                    s, t = yield from to_tokens(done, th)
                    t = yield from rope_in_place(tok_t[:, s, :], nh, hd, r, cos_, sin_, th, t)
                    slots.append(s)
                    toks.append(t)
                trs = []
                for j in (0, 2):
                    def rest(v, tr, j=j):
                        t = yield copy_either(dst[:, j:j + 2, :], v, [tr] + begin)
                        for e in evs(j):
                            e.set(t)
                        return [t]
                    trs.append((yield from transposed_pair(
                        [[tok_t[:, slots[th], (j + jj) * P:(j + jj + 1) * P] for th in range(2)] for jj in range(2)],
                        toks, rest)))
                for s in slots:
                    release(tok_ring, s, trs)

            def misc(done):
                ks, ds = [], []
                for th in range(2):
                    bank, tok = yield Need(done[th])
                    rstd, t_r = yield Need(rstd_ev)
                    r = rstd[:, th:th + 1]
                    rr = yield Need(ready["rows"])
                    k2 = kit[:, th, :].rearrange("p (a n) -> p a n", a=2)
                    a = yield DVE(ts(k2, ps[:, bank, 0:64].unsqueeze(1).to_broadcast([P, 2, 64]), r, None, ALU.mult, fast=False), [tok, t_r] + begin)
                    w_ = yield DVE(ts(wi[:, th, :], ps[:, bank, 64:72], r, 8 ** -0.5, ALU.mult, ALU.mult, fast=False), [tok, t_r] + begin)
                    o = ROWS["dt_bias"] + 16 * i
                    d = yield DVE(stt(dtv[:, th, :], ps[:, bank, 72:88], r, rows[:, o:o + 16], ALU.mult, ALU.add), [tok, t_r, rr] + begin)
                    release(MAIN, bank, [a, w_, d])
                    ds.append(d)
                    E["wi%d" % th].set(w_)
                    a = yield from rope_in_place(kit[:, th, :], 2, 64, 8, cos_i, sin_i, th, a)
                    ks.append(a)
                E["dtraw"].set(ds)

                bank, free = yield Get(SIDE)
                tr = yield PE([tp(ps[:, bank, th * P:(th + 1) * P], kit[:, th, :], ident) for th in range(2)], ks + free)
                t = yield copy_either(kiT[:, :], ps[:, bank, 0:256], [tr] + begin)
                release(SIDE, bank, [t])
                E["kiT"].set(t)

            def time_steps():
                toks = yield Need(E["dtraw"])
                n_, u_, s_, q_, m_ = (T(n, [P, 32]) for n in ("sp_n", "sp_u", "sp_s", "sp_q", "sp_m"))
                x = dtv[:, :, :].rearrange("p a n -> p (a n)")
                t = yield DVE(stt(n_[:, :], x, -1.0, x, ALU.mult, ALU.max), toks + begin)
                u = yield ACT(act(u_[:, :], n_[:, :], FN.Exp, scale=-1.0), [t] + begin)
                m = yield DVE(ts(m_[:, :], x, 0.0, None, ALU.max), toks + begin)
                t = yield DVE(ts(n_[:, :], u_[:, :], 2.0, None, ALU.add), [u])
                t = yield DVE((0.1, lambda e: e.reciprocal(n_[:, :], n_[:, :])), [t])
                t = yield DVE(tt(u_[:, :], u_[:, :], n_[:, :], ALU.mult), [t])
                sq = yield DVE(tt(s_[:, :], u_[:, :], u_[:, :], ALU.mult), [t])
                q = yield DVE(ts(q_[:, :], s_[:, :], 1.0 / 19, None, ALU.mult), [sq] + begin)
                for d in (17, 15, 13, 11, 9, 7, 5, 3):
                    q = yield DVE(stt(q_[:, :], q_[:, :], 1.0 / d, s_[:, :], ALU.add, ALU.mult), [q])
                q = yield DVE(stt(q_[:, :], q_[:, :], 1.0, u_[:, :], ALU.add, ALU.mult), [q])
                t = yield DVE(stt(x, q_[:, :], 2.0, m_[:, :], ALU.mult, ALU.add), [q, m])
                na = yield Need(ready["neg_a"])
                a2 = neg_a[:, 16 * i:16 * i + 16].unsqueeze(1).to_broadcast([P, 2, 16])
                a = yield DVE(tt(adt[:, :, :], dtv[:, :, :], a2, ALU.mult), [t, na] + begin)
                E["dt"].set(t)

                z = yield POOL((0.3, lambda e: e.memset(acs_r[:, :].bitcast(F32), 0.0)), begin)
                bank, free = yield Get(SIDE)
                o = ps[0:16, bank, 0:256]
                tr = yield PE([mm(o, adt[:, 0, :], upper, True, False),
                               mm(ps[0:16, bank, 128:256], adt[:, 1, :], upper[:, 0:128], False, True)], [a] + free)
                f = yield ACT(act(acs_f[:, :], o, FN.Copy), [tr] + begin)
                release(SIDE, bank, [f])
                hi = yield ACT(act(acs_r[0:16, 0:256], acs_f[:, :], FN.Copy), [f, z])
                lo = yield DVE(tt(acs_r[32:48, 0:256], acs_f[:, :], acs_r[0:16, 0:256].bitcast(F32), ALU.subtract), [hi, f, z])
                hi2 = yield ACT(act(acs_r[0:16, 256:384], acs_f[:, 128:256], FN.Copy), [f, z])
                lo2 = yield DVE(tt(acs_r[32:48, 256:384], acs_f[:, 128:256], acs_r[0:16, 256:384].bitcast(F32), ALU.subtract), [hi2, f, z])
                bank, free = yield Get(SIDE)
                tr = yield PE([tp(ps[:, bank, 16 * j:16 * j + 16], acs_f[:, j * P:(j + 1) * P], ident[0:16, 0:16]) for j in range(2)], [f] + free)
                n = yield ACT(act(nacs[:, :, :].rearrange("p a n -> p (a n)"), ps[:, bank, 0:32], FN.Copy, scale=-1.0), [tr] + begin)
                release(SIDE, bank, [n])
                E["acs"].set([hi, lo, hi2, lo2, n])

            def index_scores(th):
                kt = yield Need(E["kiT"])
                w = yield Need(E["wi%d" % th])
                nk = P * (th + 1)
                sc = (sc0, sc1)[th]
                t = None
                for heads in ([(0, 2, 4, 6), (1, 3, 5, 7)], [(0, 2), (1, 3), (4, 6), (5, 7)])[th]:
                    q = [(yield Need(E["qiT0"]))]
                    if heads[-1] >= 4:
                        q.append((yield Need(E["qiT1"])))
                    r, rfree = yield Get(rl_ring)
                    bank, free = yield Get(SIDE)
                    parts = []
                    for j, hh in enumerate(heads):
                        o = 64 * (hh % 2)
                        parts.append(mm(ps[:, bank, j * nk:(j + 1) * nk], qiT[o:o + 64, hh // 2, th * P:(th + 1) * P],
                                        kiT[o:o + 64, 0:nk], True, True))
                    tok = yield PE(parts, [kt] + q + free)
                    a = yield ACT(act(rl[:, r, :], ps[:, bank, :], FN.Relu, scale=0.125), [tok] + rfree)
                    release(SIDE, bank, [a])
                    for j, hh in enumerate(heads):
                        src = rl[:, r, j * nk:(j + 1) * nk]
                        if hh == 0:
                            t = yield DVE(ts(sc[:, :], src, wi[:, th, 0:1], None, ALU.mult), [a, w] + begin)
                        else:
                            t = yield DVE(stt(sc[:, :], src, wi[:, th, hh:hh + 1], sc[:, :], ALU.mult, ALU.add), [a, t, w])
                    release(rl_ring, r, [t])
                diag = sc[:, th * P:(th + 1) * P]
                t = yield POOL((0.3, lambda e: e.affine_select(out=diag, in_=diag, compare_op=ALU.is_ge, fill=FREE_KEY, base=0,
                                                               pattern=[[-1, P]], channel_multiplier=1)), [t])
                for j in range(8):
                    m = yield DVE((0.07 + nk / 960, lambda e: e.max(m8[:, th, :], sc[:, :])), [t])
                    t = yield DVE((0.07 + nk / 960, lambda e: e.match_replace(sc[:, :], m8[:, th, :], sc[:, :], TAKEN)), [m])
                bias = (bias0, bias1)[th]
                t = yield DVE(ts(bias[:, :], sc[:, :], -3.39e38, NEG, ALU.is_gt, ALU.mult), [t] + begin)
                db = bias[:, th * P:(th + 1) * P]
                t = yield POOL((0.3, lambda e: e.affine_select(out=db, in_=db, compare_op=ALU.is_ge, fill=NEG, base=0,
                                                               pattern=[[-1, P]], channel_multiplier=1)), [t])
                E["bias%d" % th].set(t)

            def head(hh):
                q = yield Need(q_ready[hh])
                k = yield Need(k_ready[hh])
                b0 = yield Need(E["bias0"])
                b1 = yield Need(E["bias1"])
                s, sfree = yield Get(pr_ring)
                m, mfree = yield Get(prs_ring)
                bank, free = yield Get(SIDE)
                tok = yield PE([mm(ps[:, bank, 0:256], qT[:, hh, 128:256], kT[:, hh, :], True, True),
                                mm(ps[:, bank, 256:384], qT[:, hh, 0:128], kT[:, hh, 0:128], True, True)], [q, k] + free)
                lo, hi = pr[:, s, 256:384], pr[:, s, 0:256]
                toks = []
                for j, (o, src, bias, bt) in enumerate(((hi, ps[:, bank, 0:256], bias1, b1), (lo, ps[:, bank, 256:384], bias0, b0))):
                    toks.append((yield DVE((0.07 + size(o) / 960, lambda e, o=o, src=src, bias=bias, j=j: e.tensor_tensor_reduce(
                        out=o, in0=src, in1=bias[:, :], op0=ALU.add, op1=ALU.min, scale=-(128 ** -0.5), scalar=3e38,
                        accum_out=prs[:, m, j:j + 1])), [tok, bt] + sfree + mfree)))
                release(SIDE, bank, toks)
                ex = []
                for j, o in enumerate((hi, lo)):
                    ex.append((yield ACT(act(o, o, FN.Exp, bias=prs[:, m, j:j + 1], scale=-1.0, accum=prs[:, m, 2 + j:3 + j]), [toks[j]])))
                r = yield DVE((0.08, lambda e: e.reciprocal(prs[:, m, 4:6], prs[:, m, 2:4])), ex)
                nr = []
                for j, o in enumerate((hi, lo)):
                    nr.append((yield DVE(ts(o, o, prs[:, m, 4 + j:5 + j], None, ALU.mult), [r])))
                release(prs_ring, m, nr)
                p, pfree = yield Get(pT_ring)
                bank, free = yield Get(SIDE)
                tr = yield PE([tp(ps[:, bank, 0:128], lo, ident), tp(ps[:, bank, 128:256], hi[:, 0:128], ident),
                               tp(ps[:, bank, 256:384], hi[:, 128:256], ident)], nr + free)
                release(pr_ring, s, [tr])
                c = yield copy_either(pT[:, p, :], ps[:, bank, 0:384], [tr] + pfree)
                release(SIDE, bank, [c])
                vt = []
                for th in range(2):
                    vt.append((yield Need(v_ready[th][hh // 4])))
                bank, free = yield Get(SIDE)
                c0 = hh * P
                tok = yield PE([mm(ps[:, bank, 0:256], v_t[:, 0, c0:c0 + P], pT[:, p, 0:256], True, False),
                                mm(ps[:, bank, 128:256], v_t[:, 1, c0:c0 + P], pT[:, p, 256:384], False, True)], [c] + vt + free)
                release(pT_ring, p, [tok])
                a = yield ACT(act(attl.hi[:, hh, :], ps[:, bank, 0:256], FN.Copy), [tok] + begin)
                l = yield DVE(tt(attl.lo[:, hh, :], ps[:, bank, 0:256], attl.hi[:, hh, :].bitcast(F32), ALU.subtract), [tok, a] + begin)
                release(SIDE, bank, [a, l])
                merged.ev(8 + hh).set([a, l])

            def conv(done, j):
                slots, toks = [], []
                for th in range(2):
                    s, t = yield from to_tokens(done, th)
                    slots.append(s)
                    toks.append(t)
                ci, cfree = yield Get(cin_ring)
                z = yield POOL((0.2, lambda e: e.memset(cin[:, :, 0:3], 0.0)), cfree)
                trs, filled = [], []
                for jj in (0, 2):
                    def rest(v, tr, jj=jj):
                        t = yield copy_either(cin[:, jj:jj + 2, 3:3 + SEQ], v, [tr] + cfree)
                        filled.append(t)
                        return [t]
                    trs.append((yield from transposed_pair(
                        [[tok_t[:, slots[th], (jj + q) * P:(jj + q + 1) * P] for th in range(2)] for q in range(2)], toks, rest)))
                for s in slots:
                    release(tok_ring, s, trs)
                if j < 2:
                    co, ofree = yield Get(cout_ring)
                    dst = cout
                else:
                    dst, ofree = bc, begin
                last = []
                for k in range(4):
                    kt = 4 * j + k
                    o = dst[:, k, :]
                    cw = lambda tap: col("conv_w", (i * 12 + kt) * 4 + tap)
                    t = yield DVE(ts(o, cin[:, k, 0:SEQ], cw(0), col("conv_b", i * 12 + kt), ALU.mult, ALU.add), [filled[k // 2], z] + ofree)
                    for tap in range(1, 4):
                        t = yield DVE(stt(o, cin[:, k, tap:tap + SEQ], cw(tap), o, ALU.mult, ALU.add), [t])
                    last.append(t)
                release(cin_ring, ci, last)
                t = yield ACT(act(dst[:, :, :], dst[:, :, :], FN.Silu), last)
                if j == 2:
                    E["bc"].set(t)
                    return
                made = []
                for th in range(2):
                    bank, free = yield Get(SIDE)
                    tr = yield PE([tp(ps[:, bank, k * P:(k + 1) * P], cout[:, k, th * P:(th + 1) * P], ident) for k in range(4)], [t] + free)
                    made.append(tr)
                    c = yield copy_either(x_t[:, th, j * 512:(j + 1) * 512], ps[:, bank, :], [tr] + begin)
                    release(SIDE, bank, [c])
                    made.append(c)
                release(cout_ring, co, made)
                E["x%d" % j].set(made)

            def scores_cb(g):
                t = yield Need(E["bc"])
                yield Need(E["bias0"])
                yield Need(E["bias1"])
                free2 = plan.ends()
                bank, free = yield Get(SIDE)
                bm, cm = bc[:, g, :], bc[:, 2 + g, :]
                tok = yield PE([mm(ps[:, bank, 0:256], bm[:, 0:128], cm, True, True),
                                mm(ps[:, bank, 256:384], bm[:, 128:256], cm[:, 128:256], True, True)], [t] + free)
                c = yield copy_either(cbT[:, g, :], ps[:, bank, 0:384], [tok] + free2)
                release(SIDE, bank, [c])
                E["cb%d" % g].set((c, free2))

            def ssd_group(g, done_z):
                acs = yield Need(E["acs"])
                t_dt = yield Need(E["dt"])
                cb, free2 = yield Need(E["cb%d" % g])
                xt_ = yield Need(E["x%d" % g])
                lr = yield Need(ready["late_r"])
                ir = yield Need(ready["ident_r"])
                hr = yield Need(ready["head_r"])
                if g == 1:
                    yield Need(E["turn"])
                y = []
                for th in range(2):
                    y.append((yield Get(SIDE)))
                for hh in range(8):
                    hd = 8 * g + hh
                    d, dfree = yield Get(dec_ring)
                    m, mfree = yield Get(mt_ring)
                    bank, free = yield Get(SIDE)
                    two = ps[:, bank, :].rearrange("p (a n) -> p a n", a=2)[:, :, 0:128]
                    tok = yield PE([mm(ps[:, bank, 0:384], head_r[:, hd:hd + 1].to_broadcast([48, P]), acs_r[:, :], True, False),
                                    mm(two, ident_r[:, :], late_r[:, :].unsqueeze(1).to_broadcast([P, 2, P]), False, True)],
                                   acs + [lr, ir, hr] + free)
                    ex, pr_ = [], []
                    for j, (c0, c1) in enumerate(((0, 256), (256, 384))):
                        a = yield ACT(act(dec[:, d, c0:c1], ps[:, bank, c0:c1], FN.Exp, bias=nacs[:, j, hd:hd + 1]), [tok] + dfree + free2)
                        ex.append(a)
                    release(SIDE, bank, ex)
                    for j, (c0, c1) in enumerate(((0, 256), (256, 384))):
                        pr_.append((yield DVE(stt(mt[:, m, c0:c1], dec[:, d, c0:c1], dtv[:, j, hd:hd + 1], cbT[:, g, c0:c1], ALU.mult, ALU.mult),
                                              [ex[j], cb, t_dt] + mfree + free2)))
                    release(dec_ring, d, pr_)
                    xs = [x_t[:, j, hd * 64:(hd + 1) * 64] for j in range(2)]
                    o = [ps[:, y[th][0], hh * 64:(hh + 1) * 64] for th in range(2)]
                    tok = yield PE([mm(o[0], mt[:, m, 0:128], xs[0], True, True),
                                    mm(o[1], mt[:, m, 128:256], xs[0], True, False),
                                    mm(o[1], mt[:, m, 256:384], xs[1], False, True)], pr_ + xt_ + (y[0][1] + y[1][1] if hh == 0 else []))
                    release(mt_ring, m, [tok])
                rr = yield Need(ready["rows"])
                yt = []
                o = ROWS["d_skip"] + 16 * i + 8 * g
                dsk = rows[:, o:o + 8].unsqueeze(2).to_broadcast([P, 8, 64])
                for th in range(2):
                    xv = x_t[:, th, g * 512:(g + 1) * 512]
                    x3 = xv.rearrange("p (h d) -> p h d", h=8)
                    t = yield DVE(tt(x3, x3, dsk, ALU.mult), [tok, rr] + xt_)
                    t = yield DVE(tt(xv, xv, ps[:, y[th][0], :], ALU.add), [t, tok])
                    release(SIDE, y[th][0], [t])
                    yt.append(t)
                E["turn"].set(t)
                sqs = []
                for th in range(2):
                    xv = x_t[:, th, g * 512:(g + 1) * 512]
                    bank, zt_tok = yield Need(done_z[th])
                    rstd, t_r = yield Need(rstd_ev)
                    s, free = yield Get(zt_ring)
                    a = yield ACT(act(zt[:, s, :], ps[:, bank, :], FN.Silu, scale=rstd[:, th:th + 1]), [zt_tok, t_r] + free + free2)
                    release(MAIN, bank, [a])
                    t = yield DVE(tt(xv, xv, zt[:, s, :], ALU.mult), [a, yt[th]])
                    yt[th] = t
                    sq = yield ACT(act(zt[:, s, :], xv, FN.Square, accum=gs[:, g, 0, th:th + 1]), [t])
                    release(zt_ring, s, [sq])
                    sqs.append(sq)
                t = yield DVE(ts(gs[:, g, 0, :], gs[:, g, 0, :], 1.0 / 512, EPS, ALU.mult, ALU.add), sqs)
                t = yield POOL(pool_pow(gs[:, g, 1, :], gs[:, g, 0, :], minus_half(2)), [t])
                for th in range(2):
                    xv = x_t[:, th, g * 512:(g + 1) * 512]
                    yt[th] = yield DVE(ts(xv, xv, gs[:, g, 1, th:th + 1], None, ALU.mult), [t, yt[th], sqs[th]])
                att_done = [merged.ev(8 + j) for j in range(8)]
                for e in att_done:
                    yield Need(e)
                free3 = plan.ends()
                for j in (0, 2):
                    k0 = 4 * g + j

                    def rest(v, tr, k0=k0):
                        last = []
                        for q in range(2):
                            k = k0 + q
                            last.append((yield ACT(act(ssd.hi[:, k, :], v[:, q, :], FN.Copy, scale=col("ssd_norm", 8 * i + k)), [tr] + free3)))
                        for q in range(2):
                            k = k0 + q
                            c = yield DVE(stt(ssd.lo[:, k, :], v[:, q, :], col("ssd_norm", 8 * i + k), ssd.hi[:, k, :].bitcast(F32),
                                              ALU.mult, ALU.subtract), [last[0], last[1]] + free3)
                            merged.ev(k).set([last[q], c])
                            last.append(c)
                        return last
                    yield from transposed_pair(
                        [[x_t[:, th, (k0 + q) * P:(k0 + q + 1) * P] for th in range(2)] for q in range(2)], yt, rest)

            merged = Both(ssd, attl)
            lhs = [(xt, 0, 0), (xt, 0, 1)]

            dz = [fresh(2), fresh(2)]
            d = fresh(2)
            spawn(heads_T(d, 8, 64, 8, cos_i, sin_i, qiT, lambda j: [E["qiT%d" % (j // 2)]]))
            yield from gemm(b["qidx"], lhs, d)
            d = fresh(2)
            spawn(misc(d))
            spawn(time_steps())
            for th in range(2):
                spawn(index_scores(th))
            yield from gemm(b["misc"], lhs, d)
            for nme, dst, evs in (("q", qT, q_ready), ("k", kT, k_ready)):
                for j in range(2):
                    d = fresh(2)
                    spawn(heads_T(d, 4, 128, 16, cos_a, sin_a, dst[:, 4 * j:4 * j + 4, :],
                                  lambda jj, evs=evs, j=j: [evs[4 * j + jj], evs[4 * j + jj + 1]]))
                    yield from gemm(b[nme, j], lhs, d)
            for j in (2, 0, 1):
                d = fresh(2)
                spawn(conv(d, j))
                if j == 2:
                    for hh in range(8):
                        spawn(head(hh))
                    for g in range(2):
                        spawn(scores_cb(g))
                        spawn(ssd_group(g, dz[g]))
                yield from gemm(b["xbc", j], lhs, d)
            for j in range(2):
                d = fresh(2)

                def v_out(j, d, th):
                    bank, tok = yield Need(d[th])
                    rstd, t_r = yield Need(rstd_ev)
                    t = yield copy_either(v_t[:, th, j * 512:(j + 1) * 512], ps[:, bank, :], [tok, t_r] + begin, scale=rstd[:, th:th + 1])
                    release(MAIN, bank, [t])
                    v_ready[th][j].set(t)
                for th in range(2):
                    spawn(v_out(j, d, th))
                yield from gemm(b["v", j], lhs, d)
            for g in range(2):
                yield from gemm(b["z", g], lhs, dz[g])
            old, before = h.renew()
            for n in range(2):
                d = fresh(2)
                for th in range(2):
                    spawn(add_back(h, old, before, n, th, d[th], 1.0), bonus=1.0)
                if n == 0:
                    then()
                yield from gemm(b["out", n], [(merged, 0, 0), (merged, 0, 1)], d)
        mod_ready = {(l, v, w): Ev() for l in range(2) for v in range(2) for w in range(2)}
        row_ready = {(l, v, w): Ev() for l in range(2) for v in range(2) for w in range(2)}
        mod_ring = Ring([0, 1])
        mod_sems = [dma_sem("mod0"), dma_sem("mod1")]
        row_sem, store_sem = dma_sem("row_in"), dma_sem("row_out")
        stores = []

        def mod_vectors(l, loaded):
            if l == 0:
                cc_ = yield Need(ready["cols"])
                for v, n in enumerate(("c", "c_ctx")):
                    t = yield ACT(act(sc_t[:, v, :], cols[:, COLS[n]:COLS[n] + 8], FN.Silu), [cc_])
                ready_sc.set(t)
            t_sc = yield Need(ready_sc)
            t_const = yield Need(ready["const"])
            acc_free = [plan.ends(), plan.ends()]
            parts = {}
            row_tok = None
            for cc in range(12):
                kind = cc // 2
                nv = 2 if l == 0 or cc < 4 else 1
                tok = [None, None]
                for k in range(8):
                    slot, arrived = yield Need(loaded[cc, k])
                    src = mod_w[:, slot, :]
                    for v in range(nv):
                        if k == 0:
                            tok[v] = yield DVE(ts(mod_acc[:, v, :], src, sc_t[:, v, 0:1], None, ALU.mult), [arrived, t_sc] + acc_free[v])
                        else:
                            tok[v] = yield DVE(stt(mod_acc[:, v, :], src, sc_t[:, v, k:k + 1], mod_acc[:, v, :], ALU.mult, ALU.add),
                                               [arrived, tok[v]])
                    release(mod_ring, slot, [t for t in tok if t])
                for v in range(nv):
                    bank, free = yield Get(SIDE)
                    if kind in (0, 1, 3, 4):
                        t = yield PE([mm(ps[:, bank, j:j + 1], mod_acc[:, v, j * P:(j + 1) * P], ones, True, True) for j in range(4)],
                                     [tok[v], t_const] + free)
                        acc_free[v] = [t]
                        kd = (0, 1, None, 2, 3)[kind]
                        b0 = COLS["b_mod"] + 48 * l + 4 * cc
                        o = 4 * (cc % 2)
                        t = yield DVE(tt(modc[:, l, v, kd, o:o + 4], ps[:, bank, 0:4], cols[:, b0:b0 + 4], ALU.add), [t])
                        release(SIDE, bank, [t])
                        parts.setdefault((v, kd), []).append(t)
                        if cc % 2 and kd % 2:
                            g = COLS["norm%d_g" % (1 + kd // 2)] + 8 * l
                            t = yield DVE(stt(gain[:, l, v, kd // 2, :], modc[:, l, v, kd, :], 1.0, cols[:, g:g + 8], ALU.add, ALU.mult),
                                          parts[v, kd])
                            mod_ready[l, v, kd // 2].set([t] + parts[v, kd - 1])
                    else:
                        t = yield PE([mm(ps[0:1, bank, :], ones, mod_acc[:, v, :], True, True)], [tok[v], t_const] + free)
                        acc_free[v] = [t]
                        c0 = 512 * (cc % 2)
                        r = yield Dma(row_sem, [(mod_row[:, :], A["b_mod_row"][l:l + 1, cc * 512:cc * 512 + 512])], [row_tok], 2048)
                        s = yield DVE(tt(mod_acc[0:1, v, :], ps[0:1, bank, :], mod_row[:, :], ALU.add), [t, r])
                        release(SIDE, bank, [s])
                        w = 0 if kind == 2 else 1
                        row_tok = yield Dma(store_sem, [(scratch[(l * 2 + v) * 2 + w:(l * 2 + v) * 2 + w + 1, c0:c0 + 512], mod_acc[0:1, v, :])], [s], 2048)
                        acc_free[v] = [row_tok]
                        stores.append(row_tok)
                        if cc % 2:
                            row_ready[l, v, w].set(row_tok)

        ready_sc = Ev()

        def mod_loader(l, loaded):
            for cc in range(12):
                for k in range(8):
                    slot, free = yield Get(mod_ring)
                    t = yield Dma(mod_sems[slot], [(mod_w[:, slot, :], A["w_mod"][l, k * P:(k + 1) * P, cc * 512:cc * 512 + 512])],
                                  free, 1 << 18)
                    loaded[cc, k].set((slot, t))

        def spawn_mod(l):
            if l == 1:
                mod_ring.free = [(i, plan.ends()) for i, _ in mod_ring.free]
            loaded = {(cc, k): Ev() for cc in range(12) for k in range(8)}
            spawn(mod_loader(l, loaded), bonus=0.0)
            spawn(mod_vectors(l, loaded), bonus=0.1)

        def prep_mod(res, l, v, which, lhs, free, rstd_ev):
            written, readers = res.written, res.readers

            def chunk(n):
                rstd, t_r = yield Need(rstd_ev)
                slots, toks = [], []
                for th in range(2):
                    t = yield Need(written[n][th])
                    s, sfree = yield Get(norm_ring)
                    t = yield DVE(ts(norm_t[:, s, :], res.tile[:, th, n * 512:(n + 1) * 512], rstd[:, th:th + 1], None, ALU.mult),
                                  [t, t_r] + sfree)
                    readers[n].append(t)
                    slots.append(s)
                    toks.append(t)
                mods = yield Need(mod_ready[l, v, which])
                trs = []
                for b in (0, 2):
                    def rest(vw, tr, b=b):
                        last = []
                        for j in range(2):
                            k = 4 * n + b + j
                            m, mfree = yield Get(modt_ring)
                            t = yield DVE(ts(mod_t[:, m, :], vw[:, j, :], gain[:, l, v, which, k:k + 1], modc[:, l, v, 2 * which, k:k + 1],
                                             ALU.mult, ALU.add, fast=False), [tr] + mods + mfree)
                            last.append(t)
                            a = yield ACT(act(lhs.hi[:, k, 0:SEQ], mod_t[:, m, :], FN.Copy), [t] + free)
                            c = yield DVE(tt(lhs.lo[:, k, 0:SEQ], mod_t[:, m, :], lhs.hi[:, k, 0:SEQ].bitcast(F32), ALU.subtract), [t, a] + free)
                            release(modt_ring, m, [a, c])
                            lhs.ev(k).set([a, c])
                        return last
                    trs.append((yield from transposed_pair(
                        [[norm_t[:, slots[th], (b + q) * P:(b + q + 1) * P] for th in range(2)] for q in range(2)], toks, rest)))
                for s in slots:
                    release(norm_ring, s, trs)
            for n in range(2):
                spawn(chunk(n), bonus=1.0)

        def room2():
            R = {}
            at = [phase]

            def T(name, shape, dt=F32, at_=None):
                R[name] = tile("r2_" + name, shape, dt, at_ or at)
                return R[name]
            T("p", [P, 3, 512])
            T("pT", [P, 2, 4, SEQ])
            T("bias", [P, 2, 640])
            o = [phase]
            T("row", [P, D], at_=o)
            T("y", [P, 2, D], at_=[mod_at])
            T("tok", [P, 4, 512])
            T("wrk", [P, 2, 512])
            T("ps_", [P, 4, 8])
            T("hn", [P, 4, 16])
            T("ln", [P, 2, 8])
            T("kt", [P, 2, 128])
            T("rg", [P, 2, 2, 2, 64])
            T("gates", [P, 4, 512])
            T("gqT", [P, 4, SEQ])
            T("gkT", [P, 512])
            T("gv", [P, 4, 128])
            T("nqT", [P, 4, SEQ])
            T("nkT", [P, 4, 512])
            T("nv", [P, 4, 512])
            o = [at[0]]
            T("n_hi", [P, 4, SEQ], F32R)
            T("n_lo", [P, 4, SEQ], F32R)
            T("cin", [P, 4, SEQ + 30], at_=o)
            T("cout", [P, 4, SEQ], at_=o)
            end = [max(at[0], o[0], limit - 16384)]
            o = [end[0]]
            T("tg", [P, 2, 512], at_=o)
            o = [end[0]]
            T("xc_hi", [P, KD, SEQ], F32R, o)
            T("xc_lo", [P, KD, SEQ], F32R, o)
            T("a_hi", [P, 4, SEQ], F32R, end)
            T("a_lo", [P, 4, SEQ], F32R, end)
            T("g_hi", [P, 4, SEQ], F32R, end)
            T("g_lo", [P, 4, SEQ], F32R, end)
            return R

        IN = dict(au=0, ag=512, nq=1024, nk=1536, nv=2048, gq=2560, gkv=3072, gate=3328)

        def mix2_blocks(l):
            w = A["w_in"]
            b = {}
            for n in ("ag", "au", "gq"):
                b[n] = block_512(w, l, 8, IN[n])
            b["gkv"] = block_256(w, l, IN["gkv"])
            for n in ("nq", "nk", "nv"):
                b[n] = block_512(w, l, 8, IN[n])
            for n in range(2):
                for i in (0, 2, 1):
                    b["gate", i, n] = block_512(w, l, 8, IN["gate"] + 1024 * i + 512 * n)
                    if i == 0:
                        b["br", 0, n] = block_512(A["w_conv_out"], l, 4, 512 * n)
                    elif i == 1:
                        b["br", 1, n] = block_512(A["w_na_out"], l, 4, 512 * n)
                    else:
                        b["br", 2, n] = block_gqa(A["w_gqa_out"], l, 512 * n)
            for n in range(2):
                b["out", n] = block_512(A["w_out"], l, 8, 512 * n)
            return b

        def kv_blocks(l):
            w = A["w_in"]
            b = {"gkv": block_256(w, l, IN["gkv"])}
            for n in ("nk", "nv"):
                b[n] = block_512(w, l, 8, IN[n])
            return b

        def mix2(l, b, xt, res, is_ctx, full, then, R):
            begin = plan.ends()
            v = 1 if is_ctx else 0
            off = 256 if is_ctx else 0
            kt0 = 2 if is_ctx else 0
            tag = f"{l}{int(is_ctx)}"

            def ring(n):
                r = Ring(list(range(n)))
                r.free = [(j, begin) for j in range(n)]
                return r
            tok_t, tok_ring = R["tok"], ring(4)
            wrk, wrk_ring = R["wrk"], ring(1)
            kt_t = R["kt"]
            p_t, p_ring = R["p"], ring(3)
            st_t, st_ring = R["ps_"], ring(4)
            pT, pT_ring = R["pT"], ring(1)
            hn, hn_ring = R["hn"], ring(4)
            rg, gates = R["rg"], R["gates"]
            E = {n: Ev() for n in ("rg", "gq0", "gq2", "gk", "nq0", "nq2", "nk0", "nk2", "conv", "gates_read", "y0", "y1", "row")}
            gv_e, nv_e = fresh(2), fresh(2)
            a_l, g_l, n_l = (Lhs(R[n + "_hi"], R[n + "_lo"]) for n in "agn")
            gate_e = {(i, n, th): Ev() for i in range(3) for n in range(2) for th in range(2)}

            def head_gains():
                rr = yield Need(ready["rows"])
                cc = yield Need(ready["const"])
                toks = []
                for q, name in enumerate(("q_g", "k_g")):
                    a = ROWS[name] + 64 * l
                    g = rows[:, a:a + 64]
                    for th in range(2):
                        co = const[:, CONST["cos"] + 64 * th:CONST["cos"] + 64 * th + 64]
                        si = const[:, CONST["sin"] + 64 * th:CONST["sin"] + 64 * th + 64]
                        t = yield DVE(tt(rg[:, q, 0, th, :], g, co, ALU.mult), [rr, cc] + begin)
                        toks.append(t)
                        t = yield DVE(tt(straight(rg[:, q, 1, th, :], [[32, 2]], 16), swapped(g, [[32, 2]], 16),
                                         straight(si, [[32, 2]], 16), ALU.mult), [rr, cc] + begin)
                        toks.append(t)
                E["rg"].set(toks)

            def head_norm(buf, nh, th, which, dst3, src_tok, out_free):
                w_, wfree = yield Get(wrk_ring)
                r_, rfree = yield Get(hn_ring)
                n = nh * 64
                b3 = buf.rearrange("p (h d) -> p h d", h=nh)
                wa, wb = wrk[:, 0, 0:n], wrk[:, 1, 0:n]
                t = yield DVE(tt(wa, buf, buf, ALU.mult), [src_tok] + wfree)
                ms, rs = hn[:, r_, 0:nh], hn[:, r_, 8:8 + nh]
                t = yield DVE((0.07 + n / 960, lambda e: e.tensor_reduce(ms, wa.rearrange("p (h d) -> p h d", h=nh), AX.X, ALU.add)), [t] + rfree)
                t = yield DVE(ts(ms, ms, 1.0 / 64, EPS, ALU.mult, ALU.add), [t])
                t = yield POOL(pool_pow(rs, ms, minus_half(nh)), [t])
                t = yield DVE(tt(b3, b3, rs.unsqueeze(2).to_broadcast([P, nh, 64]), ALU.mult), [t])
                release(hn_ring, r_, [t])
                if is_ctx:
                    rr = yield Need(ready["rows"])
                    a = ROWS[("q_g", "k_g")[which]] + 64 * l
                    gb = rows[:, a:a + 64].unsqueeze(1).to_broadcast([P, nh, 64])
                    c = yield DVE(tt(wa.rearrange("p (h d) -> p h d", h=nh), b3, gb, ALU.mult), [t, rr])
                    d = yield DVE(cp(dst3, wa.rearrange("p (g j d) -> p g j d", g=2, d=64), fast=True), [c] + out_free)
                    release(wrk_ring, w_, [d])
                    return d
                tab = yield Need(E["rg"])
                cb = rg[:, which, 0, th, :].unsqueeze(1).to_broadcast([P, nh, 64])
                c = yield DVE(tt(wa.rearrange("p (h d) -> p h d", h=nh), b3, cb, ALU.mult), [t] + tab)
                sw = []
                for hf in range(2):
                    bb, bw, bs = buf[:, 32 * hf:n], wb[:, 32 * hf:n], rg[:, which, 1, th, 32 * hf:32 * hf + 32]
                    sb_ = bass.AP(bs.tensor, bs.offset, ap=[list(bs.ap[0]), [0, nh], [16, 2], [1, 16]])
                    sw.append((yield DVE(tt(straight(bw, [[64, nh]], 16), swapped(bb, [[64, nh]], 16), sb_, ALU.mult), [t] + tab + wfree)))
                v4 = "p (g j d) -> p g j d"
                d = yield DVE(tt(dst3, wa.rearrange(v4, g=2, d=64), wb.rearrange(v4, g=2, d=64), ALU.add), [c] + sw + out_free)
                release(wrk_ring, w_, [d])
                return d

            def take(done, th, scale=None):
                bank, tok = yield Need(done[th])
                s, free = yield Get(tok_ring)
                t = yield copy_either(tok_t[:, s, :], ps[:, bank, :], [tok] + free, scale=scale)
                release(MAIN, bank, [t])
                return s, t

            def tok_pairs(slots, toks, place_, evs):
                trs = []
                for j in (0, 2):
                    def rest(vw, tr, j=j):
                        t = yield from place_(j, vw, tr)
                        evs[j // 2].set(t)
                        return [t]
                    trs.append((yield from transposed_pair(
                        [[tok_t[:, slots[th], (j + q) * P:(j + q + 1) * P] for th in range(2)] for q in range(2)], toks, rest)))
                for s in slots:
                    release(tok_ring, s, trs)

            def conv_branch(dg, du):
                tg = R["tg"]
                slots, toks = [], []
                gt = []
                for th in range(2):
                    bank, tok = yield Need(dg[th])
                    t = yield ACT(act(tg[:, th, :], ps[:, bank, :], FN.Tanh, scale=0.5), [tok] + begin)
                    release(MAIN, bank, [t])
                    gt.append(t)
                zs = []
                for o in (0, SEQ + 15):
                    zs.append((yield POOL((0.2, lambda e, o=o: e.memset(R["cin"][:, :, o:o + 15], 0.0)), begin)))
                for th in range(2):
                    bank, tok = yield Need(du[th])
                    s, free = yield Get(tok_ring)
                    t = yield DVE(stt(tok_t[:, s, :], tg[:, th, :], 1.0, ps[:, bank, :], ALU.add, ALU.mult), [tok, gt[th]] + free)
                    release(MAIN, bank, [t])
                    slots.append(s)
                    toks.append(t)
                tg_read = list(toks)
                ev = fresh(2)
                cin, cout = R["cin"], R["cout"]

                def place_(j, vw, tr):
                    t = yield ACT(act(cin[:, j:j + 2, 15:15 + SEQ], vw, FN.Copy, scale=0.5), [tr] + begin)
                    return t
                yield from tok_pairs(slots, toks, place_, ev)
                last = []
                for k in range(4):
                    e = yield Need(ev[k // 2])
                    o = cout[:, k, :]
                    w0 = (l * 4 + k) * 31
                    t = yield DVE(ts(o, cin[:, k, 0:SEQ], col("conv2_w", w0), col("conv2_b", 4 * l + k), ALU.mult, ALU.add), [e] + zs + begin)
                    for tap in range(1, 31):
                        t = yield DVE(stt(o, cin[:, k, tap:tap + SEQ], col("conv2_w", w0 + tap), o, ALU.mult, ALU.add), [t])
                    last.append(t)
                slots, toks = [], []
                ln = R["ln"]
                conv_read = []
                for th in range(2):
                    s, sfree = yield Get(tok_ring)
                    w_, wfree = yield Get(wrk_ring)
                    bank, free = yield Get(SIDE)
                    tr = yield PE([tp(ps[:, bank, k * P:(k + 1) * P], cout[:, k, th * P:(th + 1) * P], ident) for k in range(4)], last + free)
                    conv_read.append(tr)
                    bs = wrk[:, 0, 0:6]
                    t = yield DVE((0.6, lambda e: e.bn_stats(bs, ps[:, bank, :])), [tr] + wfree)
                    t = yield DVE((0.1, lambda e, th=th: e.bn_aggr(ln[:, th, 0:2], bs)), [t] + begin)
                    release(wrk_ring, w_, [t])
                    t = yield DVE(ts(ln[:, th, 2:3], ln[:, th, 1:2], EPS, None, ALU.add), [t])
                    t = yield POOL(pool_pow(ln[:, th, 3:4], ln[:, th, 2:3], minus_half(1)), [t])
                    t = yield DVE(ts(tok_t[:, s, :], ps[:, bank, :], ln[:, th, 0:1], ln[:, th, 3:4], ALU.subtract, ALU.mult, fast=False), [t, tr] + sfree)
                    release(SIDE, bank, [t])
                    slots.append(s)
                    toks.append(t)
                E["conv"].set(conv_read)
                ev = fresh(2)

                def place2(j, vw, tr):
                    for q in range(2):
                        k = j + q
                        s, free = yield Get(modt_ring)
                        x = mod_t[:, s, :]
                        t = yield ACT(act(x, vw[:, q, :], FN.Silu, bias=col("ln_b", 4 * l + k), scale=col("ln_g", 4 * l + k)), [tr] + free)
                        hi, lo = a_l.hi[:, k, :], a_l.lo[:, k, :]
                        a = yield ACT(act(hi, x, FN.Copy), [t] + begin + tg_read)
                        c = yield DVE(tt(lo, x, hi.bitcast(F32), ALU.subtract), [t, a] + begin + tg_read)
                        release(modt_ring, s, [a, c])
                        a_l.ev(k).set([a, c])
                    return t
                yield from tok_pairs(slots, toks, place2, ev)

            def gq_job(done):
                slots, toks = [], []
                for th in range(2):
                    s, t = yield from take(done, th)
                    dst = tok_t[:, s, :].rearrange("p (j g d) -> p g j d", j=4, g=2)
                    t = yield from head_norm(tok_t[:, s, :], 8, th, 0, dst, t, [])
                    slots.append(s)
                    toks.append(t)

                def place_(j, vw, tr):
                    return (yield copy_either(R["gqT"][:, j:j + 2, :], vw, [tr] + begin))
                yield from tok_pairs(slots, toks, place_, [E["gq0"], E["gq2"]])

            def kv_job(done):
                toks = []
                for th in range(2):
                    bank, tok = yield Need(done[th])
                    a = yield copy_either(kt_t[:, th, :], ps[:, bank, 0:128], [tok] + begin)
                    c = yield copy_either(R["gv"][:, kt0 + th, :], ps[:, bank, 128:256], [tok, a] + begin)
                    release(MAIN, bank, [a, c])
                    gv_e[th].set(c)
                    d3 = kt_t[:, th, :].rearrange("p (j g d) -> p g j d", j=1, g=2)
                    toks.append((yield from head_norm(kt_t[:, th, :], 2, th, 1, d3, a, [])))
                bank, free = yield Get(SIDE)
                tr = yield PE([tp(ps[:, bank, th * P:(th + 1) * P], kt_t[:, th, :], ident) for th in range(2)], toks + free)
                t = yield copy_either(R["gkT"][:, off:off + 256], ps[:, bank, 0:256], [tr] + begin)
                release(SIDE, bank, [t])
                E["gk"].set(t)

            def nqk_job(done, dst, o, scale, evs):
                slots, toks = [], []
                for th in range(2):
                    s, t = yield from take(done, th)
                    slots.append(s)
                    toks.append(t)

                def place_(j, vw, tr):
                    return (yield copy_either(dst[:, j:j + 2, o:o + SEQ], vw, [tr] + begin, scale=scale))
                yield from tok_pairs(slots, toks, place_, evs)

            def nv_job(done, th):
                bank, tok = yield Need(done[th])
                t = yield copy_either(R["nv"][:, kt0 + th, :], ps[:, bank, :], [tok] + begin)
                release(MAIN, bank, [t])
                nv_e[th].set(t)

            nk_keys = 256 if is_ctx else 512

            def softmaxed(q, k, toks, bias, scale, out_T, th, T_free, ev):
                s, sfree = yield Get(p_ring)
                m, mfree = yield Get(st_ring)
                bank, free = yield Get(SIDE)
                tok = yield PE([mm(ps[:, bank, 0:nk_keys], q, k, True, True)], toks + free)
                pv = p_t[:, s, 0:nk_keys]
                x = ps[:, bank, 0:nk_keys]
                st = lambda j: st_t[:, m, j:j + 1]
                if bias is None:
                    t = yield DVE((0.07 + nk_keys / 960, lambda e: e.tensor_reduce(st(0), x, AX.X, ALU.max)), [tok] + mfree)
                    t = yield DVE(ts(st(1), st(0), -scale, None, ALU.mult), [t])
                    e_ = yield ACT(act(pv, x, FN.Exp, bias=st(1), scale=scale, accum=st(2)), [t, tok] + sfree)
                    release(SIDE, bank, [t, e_])
                else:
                    b_ap, b_toks = bias
                    p2 = pv.rearrange("p (a n) -> p a n", a=2)
                    x2 = x.rearrange("p (a n) -> p a n", a=2)
                    t = yield DVE((0.07 + nk_keys / 960, lambda e: e.tensor_tensor_reduce(
                        out=p2, in0=x2, in1=b_ap, op0=ALU.add, op1=ALU.min, scale=-1.0, scalar=3e38, accum_out=st(1))), [tok] + b_toks + sfree + mfree)
                    release(SIDE, bank, [t])
                    e_ = yield ACT(act(pv, pv, FN.Exp, bias=st(1), scale=-1.0, accum=st(2)), [t])
                r = yield DVE((0.08, lambda e: e.reciprocal(st(3), st(2))), [e_])
                r = yield DVE(ts(pv, pv, st(3), None, ALU.mult), [r])
                release(st_ring, m, [r])
                n = nk_keys // P
                bank2, free = yield Get(SIDE)
                tr = yield PE([tp(ps[:, bank2, j * P:(j + 1) * P], p_t[:, s, j * P:(j + 1) * P], ident) for j in range(n)], [r] + free)
                release(p_ring, s, [tr])
                c = yield copy_either(out_T[:, 0:n, th * P:(th + 1) * P], ps[:, bank2, 0:n * P].rearrange("p (k t) -> p k t", k=n), [tr] + T_free)
                release(SIDE, bank2, [c])
                ev.set((c, r, t))

            def pair(kind, j):
                if kind == "g":
                    q_t, k_t, v_t, lhs = R["gqT"], R["gkT"][:, :], R["gv"], g_l
                    q_ev = yield Need(E["gq0"] if j < 2 else E["gq2"])
                    k_ev = yield Need(E["gk"])
                    ve = gv_e
                    vc = [0, 64]
                else:
                    q_t, k_t, v_t, lhs = R["nqT"], R["nkT"][:, j, :], R["nv"], n_l
                    q_ev = yield Need(E["nq0"] if j < 2 else E["nq2"])
                    k_ev = yield Need(E["nk0"] if j < 2 else E["nk2"])
                    ve = nv_e
                    vc = [128 * j, 128 * j + 64]
                pt, tfree = yield Get(pT_ring)
                evs = {}
                for g in range(2):
                    bias_slot = None
                    if kind == "n" and not is_ctx:
                        bias_slot, b_toks = yield Need(bias_e[2 * j + g])
                    for th in range(2):
                        evs[g, th] = Ev()
                        bias = None
                        if bias_slot is not None:
                            st_ = 128 * (1 - th)
                            base = R["bias"][:, bias_slot, :]
                            bias = (bass.AP(base.tensor, base.offset + st_, ap=[list(base.ap[0]), [384 - st_, 2], [1, 256]]), b_toks)
                        scale = 0.125 if kind == "g" or is_ctx else 1.0
                        if kind == "n":
                            scale = 1.0
                        k_ap = k_t[64 * g:64 * g + 64, (256 if is_ctx else 0):512]
                        spawn(softmaxed(q_t[64 * g:64 * g + 64, j, th * P:(th + 1) * P], k_ap, [q_ev, k_ev] + begin, bias, scale,
                                        pT[:, g, :, :], th, tfree, evs[g, th]))
                    if bias_slot is not None:
                        spawn(give_back(bias_slot, evs[g, 0], evs[g, 1]))
                toks = []
                for key in evs:
                    x = yield Need(evs[key])
                    toks.append(x[0])
                for e in ve:
                    toks.append((yield Need(e)))
                bank, free = yield Get(SIDE)
                parts = []
                n = nk_keys // P
                for kt in range(n):
                    for g in range(2):
                        parts.append(mm(ps[64 * g:64 * g + 64, bank, 0:256], v_t[:, (2 if is_ctx else 0) + kt, vc[g]:vc[g] + 64],
                                        pT[:, g, kt, :], kt == 0, kt == n - 1))
                tok = yield PE([(p_[0] * 0.5, p_[1]) for p_ in parts], toks + free)
                release(pT_ring, pt, [tok])
                extra = (yield Need(E["conv"])) if kind == "n" else []
                hi, lo = lhs.hi[:, j, :], lhs.lo[:, j, :]
                a = yield ACT(act(hi, ps[:, bank, 0:256], FN.Copy), [tok] + begin + extra)
                c = yield DVE(tt(lo, ps[:, bank, 0:256], hi.bitcast(F32), ALU.subtract), [tok, a] + begin + extra)
                release(SIDE, bank, [a, c])
                lhs.ev(j).set([a, c])

            bias_e = fresh(8)
            bias_ring = ring(2)

            def give_back(slot, e0, e1):
                a = yield Need(e0)
                c = yield Need(e1)
                release(bias_ring, slot, [a[2], c[2]])

            def bias_loader():
                zs = []
                for s in range(2):
                    zs.append((yield POOL((0.3, lambda e, s=s: e.memset(R["bias"][:, s, 384:640], 0.0)), begin)))
                sems_ = bias_sems
                for hh in range(8):
                    s, free = yield Get(bias_ring)
                    t = yield Dma(sems_[s], [(R["bias"][:, s, 0:384], A["na_table"][l, :, hh, :])], free, 128 * 384 * 4)
                    bias_e[hh].set((s, [t] + zs))

            gate_ring = ring(4)

            def gate_job(i, n, th, done):
                bank, tok = yield Need(done[th])
                s, free = yield Get(gate_ring)
                t = yield ACT(act(gates[:, s, :], ps[:, bank, :], FN.Tanh, scale=0.5), [tok] + free)
                release(MAIN, bank, [t])
                gate_e[i, n, th].set((s, t))
            y_e = {(n, th): Ev() for n in range(2) for th in range(2)}

            def branch_job(n, th, dones):
                y = R["y"][:, th, n * 512:(n + 1) * 512]
                t = None
                for i in (0, 2, 1):
                    bank, tok = yield Need(dones[i][th])
                    slot, g_tok = yield Need(gate_e[i, n, th])
                    x = ps[:, bank, :]
                    r = yield DVE(stt(y if i == 0 else x, gates[:, slot, :], 1.0, x, ALU.add, ALU.mult), [tok, g_tok] + (begin if i == 0 else []))
                    release(gate_ring, slot, [r])
                    t = r if i == 0 else (yield DVE(tt(y, y, x, ALU.add), [r, t]))
                    release(MAIN, bank, [t])
                y_e[n, th].set(t)

            def y_job(n, ylhs, last_read):
                f = yield Need(last_read)
                ylhs.free = f
                toks = []
                for th in range(2):
                    toks.append((yield Need(y_e[n, th])))
                for j in (0, 2):
                    k = 4 * n + j
                    yield from transposed_pair([[R["y"][:, th, (k + q) * P:(k + q + 1) * P] for th in range(2)] for q in range(2)],
                                               toks, split_rest(ylhs, k, 0, scale=0.5))

            lhs = [(xt, 0, 0), (xt, 0, 1)]
            if not is_ctx:
                spawn(head_gains())
            if full:
                dg, du = fresh(2), fresh(2)
                spawn(conv_branch(dg, du))
                yield from gemm(b["ag"], lhs, dg)
                yield from gemm(b["au"], lhs, du)
                d = fresh(2)
                spawn(gq_job(d))
                yield from gemm(b["gq"], lhs, d)
            d = fresh(2)
            spawn(kv_job(d))
            yield from gemm(b["gkv"], lhs, d)
            if full:
                for j in range(4):
                    spawn(pair("g", j))
                d = fresh(2)
                spawn(nqk_job(d, R["nqT"], 0, 0.125, [E["nq0"], E["nq2"]]))
                yield from gemm(b["nq"], lhs, d)
            d = fresh(2)
            spawn(nqk_job(d, R["nkT"], off, None, [E["nk0"], E["nk2"]]))
            yield from gemm(b["nk"], lhs, d)
            d = fresh(2)
            for th in range(2):
                spawn(nv_job(d, th))
            if full:
                if not is_ctx:
                    spawn(bias_loader())
                for j in range(4):
                    spawn(pair("n", j))
            yield from gemm(b["nv"], lhs, d)
            if not full:
                for e in (E["gk"], E["nk0"], E["nk2"], *gv_e, *nv_e):
                    yield Need(e)
                return
            ylhs = Lhs(xt_hi, xt_lo)
            last_read = Ev()
            gone = Ev()
            branch_lhs = (a_l, n_l, g_l)

            def attention_gone():
                for x in (n_l, g_l):
                    for j in range(4):
                        yield Need(x.ev(j))
                gone.set(plan.ends())
            spawn(attention_gone())
            for n in range(2):
                dones = [fresh(2) for _ in range(3)]
                for th in range(2):
                    spawn(branch_job(n, th, dones))
                spawn(y_job(n, ylhs, last_read))
                for i in (0, 2, 1):
                    d = fresh(2)
                    for th in range(2):
                        spawn(gate_job(i, n, th, d))
                    yield from gemm(b["gate", i, n], lhs, d)
                    if n == 1 and i == 1:
                        last_read.set([plan.last["PE"]])
                    x = branch_lhs[i]
                    yield from gemm(b["br", i, n], [(x, 0, 0), (x, 0, 1)], dones[i])
            free4 = yield Need(gone)

            def row_job():
                t = yield Need(row_ready[l, v, 0])
                r0 = (l * 2 + v) * 2
                t = yield Dma(rowload_sem, [(R["row"][:, :], bass.AP(scratch.tensor, r0 * D, ap=[[0, P], [1, D]]))], [t] + free4, 1 << 19)
                E["row"].set(t)
            spawn(row_job(), bonus=2.0)
            t_row = yield Need(E["row"])
            old, before = res.renew()
            for n in range(2):
                d = fresh(2)
                for th in range(2):
                    spawn(add_back(res, old, before, n, th, d[th], None, (R["row"], t_row)), bonus=1.0)
                if n == 0 and then:
                    then()
                yield from gemm(b["out", n], [(ylhs, 0, 0), (ylhs, 0, 1)], d)

        bias_sems = [dma_sem("bias0"), dma_sem("bias1")]
        rowload_sem = dma_sem("row_load")

        def ffn_blocks(w_in, w_out, l, parts):
            a = []
            down = []
            for c0, c1 in parts:
                for c in range(c0, c1):
                    a.append(block_pair(w_in, l, 256 * c, FF + 256 * c))
                down.append([block_512(w_out, l, 2 * (c1 - c0), 512 * n, 2 * c0) for n in range(2)])
            return a, down

        ONE, TWO = [(0, 11)], [(0, 6), (6, 11)]
        F = {}
        for i in range(2):
            F["f1", i] = ffn_blocks(A["w_ffn1_in"], A["w_ffn1_out"], i, ONE)
            F["mix", i] = mix1_blocks(i)
            F["f2", i] = ffn_blocks(A["w_ffn2_in"], A["w_ffn2_out"], i, ONE)
        F["c0"] = mix2_blocks(0)
        F["x0"] = mix2_blocks(0)
        F["g0"] = ffn_blocks(A["w_ffn_in"], A["w_ffn_out"], 0, TWO)
        F["c1"] = kv_blocks(1)
        F["x1"] = mix2_blocks(1)
        F["g1"] = ffn_blocks(A["w_ffn_in"], A["w_ffn_out"], 1, ONE)

        def normed(res, name, dst, sem, row_t, rows_free, written_evs=None):
            rs = stats(res)
            written, readers = res.written, res.readers

            def go():
                t_row = yield Dma(sem, [(row_t[:, :], bass.AP(A[name].tensor, 0, ap=[[0, P], [1, D]]))], rows_free, 1 << 19)
                rstd, t_r = yield Need(rs)
                for n in range(2):
                    for th in range(2):
                        t = yield Need(written[n][th])
                        s = slice(n * 512, (n + 1) * 512)
                        t = yield DVE(stt(dst[:, th, s], res.tile[:, th, s], rstd[:, th:th + 1], row_t[:, s], ALU.mult, ALU.mult),
                                      [t, t_r, t_row] + readers[n])
                        written_evs[n][th].set(t)
            spawn(go(), bonus=1.0)

        row_sem2 = dma_sem("gain_row")
        final = []

        def main():
            S = {}
            for i in range(2):
                def scaled(name):
                    def then():
                        S["lhs"] = Lhs(xt_hi, xt_lo)
                        free = [plan.last["PE"]] if "PE" in plan.last else []
                        S["rs"] = stats(h)
                        prep_scaled(h, (name, 8 * S["i"]), S["lhs"], free)
                    return then
                S["i"] = i
                if i == 0:
                    scaled("norm_ffn1")()
                plan.stage += 1
                yield from ffn(*F["f1", i], [(S["lhs"], 0, h, S["rs"], 0.5, None)], ONE, f"a{i}", scaled("norm_mix"))
                plan.stage += 1
                yield from mix1(i, F["mix", i], S["lhs"], S["rs"], scaled("norm_ffn2"))
                plan.stage += 1
                if i == 1:
                    spawn(ctx_start(plan.ends()))
                    S["ctx_rs"] = stats(hc)

                def after(i=i):
                    if i == 0:
                        S["i"] = 1
                        scaled("norm_ffn1")()
                    else:
                        S["lhs"] = Lhs(xt_hi, xt_lo)
                        free = [plan.last["PE"]]
                        prep_mod(hc, 0, 1, 0, S["lhs"], free, S["ctx_rs"])
                yield from ffn(*F["f2", i], [(S["lhs"], 0, h, S["rs"], 0.5, None)], ONE, f"b{i}", after)
            R = room2()
            old_h = h.written
            evs = [fresh(2), fresh(2)]
            row_t = tile("final_row", [P, D], F32, [mod_at])
            normed(h, "final_norm", h_t, row_sem2, row_t, plan.ends(), evs)
            h_readers = h.readers
            h.written = evs
            h.readers = [[], []]
            plan.stage += 1
            yield from mix2(0, F["c0"], S["lhs"], hc, True, True, None, R)
            S["lhs"] = Lhs(xt_hi, xt_lo)
            prep_mod(h, 0, 0, 0, S["lhs"], [plan.last["PE"]], stats(h))
            plan.stage += 1

            def then_ffn():
                S["cl"] = Lhs(R["xc_hi"], R["xc_lo"])
                prep_mod(hc, 0, 1, 1, S["cl"], plan.ends(), stats(hc))
                S["xl"] = Lhs(xt_hi, xt_lo)
                S["x_rs"] = stats(h)
                S["x_prep"] = True
            yield from mix2(0, F["x0"], S["lhs"], h, False, True, then_ffn, R)
            prep_mod(h, 0, 0, 1, S["xl"], [plan.last["PE"]], S["x_rs"])
            spawn_mod(1)
            plan.stage += 1
            g_rows, g_toks = [], []
            for v in (0, 1):
                t_ = tile(f"g2_{v}", [P, D], F32, [limit - 16384 - 4096 * (v + 1)])
                ev = Ev()

                def load(v=v, t_=t_, ev=ev, free=plan.ends()):
                    t = yield Need(row_ready[0, v, 1])
                    t = yield Dma(rowload_sem, [(t_[:, :], bass.AP(scratch.tensor, (v * 2 + 1) * D, ap=[[0, P], [1, D]]))], [t] + free, 1 << 19)
                    ev.set(t)
                spawn(load())
                g_rows.append(t_)
                g_toks.append((yield Need(ev)))

            def then_1():
                S["cl"] = Lhs(R["xc_hi"], R["xc_lo"])
                S["c_rs"] = stats(hc)
                prep_mod(hc, 1, 1, 0, S["cl"], [plan.last["PE"]], S["c_rs"])
                S["xl"] = Lhs(xt_hi, xt_lo)
                prep_mod(h, 1, 0, 0, S["xl"], [plan.last["PE"]], stats(h))
            yield from ffn(*F["g0"], [(S["xl"], 0, h, None, None, (g_rows[0], g_toks[0])), (S["cl"], 0, hc, None, None, (g_rows[1], g_toks[1]))],
                           TWO, "c0", then_1)
            plan.stage += 1
            yield from mix2(1, F["c1"], S["cl"], hc, True, False, None, R)
            plan.stage += 1

            def then_2():
                S["x_rs"] = stats(h)
            yield from mix2(1, F["x1"], S["xl"], h, False, True, then_2, R)
            S["xl"] = Lhs(xt_hi, xt_lo)
            prep_mod(h, 1, 0, 1, S["xl"], [plan.last["PE"]], S["x_rs"])
            plan.stage += 1
            ev = Ev()

            def load2(free=plan.ends()):
                t = yield Need(row_ready[1, 0, 1])
                t = yield Dma(rowload_sem, [(g_rows[0][:, :], bass.AP(scratch.tensor, 5 * D, ap=[[0, P], [1, D]]))], [t] + free, 1 << 19)
                ev.set(t)
            spawn(load2())
            t2 = yield Need(ev)
            out_t = tile("out_t", [P, 2, D], F32, [limit - 16384])
            row_f = tile("final_row2", [P, D], F32, [limit - 16384 - 8192])
            evs = [fresh(2), fresh(2)]

            def then_out():
                normed(h, "final_g", out_t, row_sem2, row_f, plan.ends(), evs)
            yield from ffn(*F["g1"], [(S["xl"], 0, h, None, None, (g_rows[0], t2))], ONE, "c1", then_out)
            for n in range(2):
                for th in range(2):
                    t = yield Need(evs[n][th])
                    final.append((yield Dma(out_sems[2 * n + th], [(out[th * P:(th + 1) * P, n * 512:(n + 1) * 512],
                                                       out_t[:, th, n * 512:(n + 1) * 512])], [t], 1 << 18)))

        out_sems = [dma_sem(f"out{j}") for j in range(4)]

        ctx_sem = dma_sem("in_ctx")

        def ctx_start(free):
            t = yield Dma(ctx_sem, [(hc_t[:, :, :], A["ctx"].rearrange("(t p) n -> p t n", p=P))], free, 1 << 20)
            for n in range(2):
                for th in range(2):
                    hc.written[n][th].set(t)

        spawn(setup(), bonus=3.0)
        spawn(setup_x(), bonus=3.0)
        spawn(loader(), bonus=0.8)
        spawn(splitter(), bonus=0.7)
        spawn(setup_small())
        spawn(rope_tables())
        spawn(main(), bonus=0.0)
        spawn_mod(0)
        plan.run()
        plan.emit(nc, sem_of, stores + final)
        return plan


def layout(i):
    f = np.float32

    def per_feature(a):
        a = np.asarray(a)
        return a.reshape(-1, P).T

    def taps(a, n):
        a = np.asarray(a)
        return a.reshape(2, a.shape[1], n, P).transpose(3, 0, 2, 1).reshape(P, -1)

    cols = np.concatenate([per_feature(i["norm_ffn1"]), per_feature(i["norm_mix"]), per_feature(i["norm_ffn2"]),
                           per_feature(i["ssd_norm"]), taps(i["conv_w"], 12), per_feature(i["conv_b"]),
                           per_feature(i["norm1_g_2"]), per_feature(i["norm2_g_2"]), per_feature(i["b_mod_2"]),
                           taps(i["conv_w_2"], 4), per_feature(i["conv_b_2"]), per_feature(i["conv_ln_g_2"]),
                           per_feature(i["conv_ln_b_2"]), per_feature(i["c_2"]), per_feature(i["c_ctx_2"])], axis=1)
    rows = np.concatenate([np.asarray(i[n]).reshape(-1) for n in ("dt_bias", "a_log", "d_skip", "q_norm_g_2", "k_norm_g_2")])[None]

    s, l = np.arange(P)[:, None], np.arange(P)[None]
    const = np.zeros((P, N_CONST), f)

    def put(name, a):
        const[:a.shape[0], CONST[name]:CONST[name] + a.shape[1]] = a
    put("ident", np.eye(P, dtype=f))
    put("upper", np.concatenate([(s <= l).astype(f), np.ones((P, P), f)], 1))
    put("late", np.where(l < s, f(NEG), f(0)))
    head = np.zeros((48, 16), f)
    head[:16] = head[32:] = np.eye(16, dtype=f)
    put("head", head)
    freq = (f(500000.0) ** (-np.arange(0, 32, 2, dtype=f) / f(32))).astype(f)
    put("freq", np.tile(freq, (P, 1)))
    t = np.arange(SEQ)
    fr = (f(10000.0) ** (-np.arange(0, 32, 2, dtype=f) / f(32))).astype(f)
    ang = np.stack([(t // 64).astype(f)[:, None] * fr, (t % 64).astype(f)[:, None] * fr], 1)
    co, si = np.cos(ang.astype(np.float64)), np.sin(ang.astype(np.float64))
    co = np.stack([co, co], 2).reshape(2, P, 64).transpose(1, 0, 2).reshape(P, 128)
    si = np.stack([-si, si], 2).reshape(2, P, 64).transpose(1, 0, 2).reshape(P, 128)
    put("cos", co.astype(f))
    put("sin", si.astype(f))
    put("one", np.ones((P, 1), f))
    put("half", np.full((P, 8), -0.5, f))

    rpb = np.asarray(i["na_rpb_2"]).reshape(2, 8, -1)
    with_neg = np.concatenate([rpb, np.full((2, 8, 1), NEG, f)], axis=2)
    rr, c, j, kc = np.ogrid[0:2, 0:64, 0:6, 0:64]
    w0 = np.clip(c - 8, 0, 48)
    dist = np.clip(kc - c + 15, 0, 30)
    at = np.where((kc >= w0) & (kc < w0 + 16), (5 - rr + j) * 31 + dist, 15 * 31).reshape(P, 384)
    table = np.ascontiguousarray(with_neg[:, :, at].transpose(0, 2, 1, 3))
    return {"cols": np.ascontiguousarray(cols), "rows": np.ascontiguousarray(rows), "const": const, "na_table": table,
            "pos": np.ascontiguousarray(np.asarray(i["positions"]).reshape(2, P).T),
            "x": np.asarray(i["x"])[0], "ctx": np.asarray(i["ctx_2"])[0],
            "final_norm": np.asarray(i["final_norm"])[None], "final_g": np.asarray(i["final_g_2"])[None],
            "b_mod_row": np.asarray(i["b_mod_2"]),
            "w_ffn1_in": i["w_ffn1_in"], "w_ffn1_out": i["w_ffn1_out"], "w_mix_in": i["w_mix_in"],
            "w_mix_out": i["w_mix_out"], "w_ffn2_in": i["w_ffn2_in"], "w_ffn2_out": i["w_ffn2_out"],
            "w_mod": i["w_mod_2"], "w_in": i["w_in_2"], "w_conv_out": i["w_conv_out_2"], "w_na_out": i["w_na_out_2"],
            "w_gqa_out": i["w_gqa_out_2"], "w_out": i["w_out_2"], "w_ffn_in": i["w_ffn_in_2"], "w_ffn_out": i["w_ffn_out_2"]}


def build(nc, arrays):
    A = {n: nc.dram_tensor("in_" + n, list(a.shape), mybir.dt.from_np(a.dtype), kind="ExternalInput").ap()
         for n, a in arrays.items()}
    out = nc.dram_tensor("out", [SEQ, D], F32, kind="ExternalOutput").ap()
    scratch = nc.dram_tensor("mod_rows", [8, D], F32).ap()
    return program(nc, A, out, scratch)


def kernel(**inputs):
    import concourse.bacc as _bacc
    from concourse.bass_utils import run_bass_kernel_spmd as _run

    arrays = {n: np.ascontiguousarray(a) for n, a in layout(inputs).items()}
    nc = _bacc.Bacc("TRN2", target_bir_lowering=False, num_devices=1, dynamic_dma_scratch_size=64)
    build(nc, arrays)
    r = _run(nc, [{"in_" + n: a for n, a in arrays.items()}], core_ids=[0])
    return r.results[0]["out"][None]
```
